# Optimizing a Trainium2 kernel written in Bass

```python
import jax, jax.numpy as jnp
from jax import lax
import numpy as np

D_MODEL = 2048
BATCH = 1
SEQ = 256
DEPTH = 2

N_MIXERS = 2
FOX_HEADS = 16
FOX_HEAD_DIM = D_MODEL // FOX_HEADS
RET_HEADS = 8
RET_QK_DIM = D_MODEL // RET_HEADS
RET_V_DIM = 2 * RET_QK_DIM
D_FF = 4 * D_MODEL
Q_BLOCK = 128
RET_CHUNK = 128
RMS_EPS = 1e-6
ROPE_BASE = 10000.0
N_FOX = (DEPTH + 1) // 2
N_RET = DEPTH // 2

kernel_name = "fox_retnet_hybrid_trunk"

def rmsnorm(x, g):
    x32 = x.astype(jnp.float32)
    y = x32 * lax.rsqrt(jnp.mean(jnp.square(x32), axis=-1, keepdims=True) + RMS_EPS)
    return (y * g.astype(jnp.float32)).astype(x.dtype)

def fox_mixer(h, wq, wk, wv, wf, bf, wo):
    B, S, _ = h.shape
    H, dh = FOX_HEADS, FOX_HEAD_DIM

    def heads(w):
        return (h @ w).reshape(B, S, H, dh).transpose(0, 2, 1, 3).astype(jnp.float32)

    q = heads(wq) * (dh ** -0.5)
    k = heads(wk)
    v = heads(wv)
    log_f = jax.nn.log_sigmoid((h @ wf + bf).astype(jnp.float32))
    c = jnp.cumsum(log_f, axis=1).transpose(0, 2, 1)

    nb = S // Q_BLOCK
    q_blocks = q.reshape(B, H, nb, Q_BLOCK, dh).transpose(2, 0, 1, 3, 4)
    c_blocks = c.reshape(B, H, nb, Q_BLOCK).transpose(2, 0, 1, 3)
    k_pos = jnp.arange(S)

    def one_block(args):
        qi, ci, bi = args
        q_pos = bi * Q_BLOCK + jnp.arange(Q_BLOCK)
        logits = jnp.einsum('bhqd,bhkd->bhqk', qi, k) + ci[..., None] - c[:, :, None, :]
        logits = jnp.where(k_pos[None, :] <= q_pos[:, None], logits, -jnp.inf)
        p = jax.nn.softmax(logits, axis=-1)
        return jnp.einsum('bhqk,bhkd->bhqd', p, v)

    o = lax.map(one_block, (q_blocks, c_blocks, jnp.arange(nb)))
    o = o.transpose(1, 0, 3, 2, 4).reshape(B, S, H * dh)
    return o.astype(h.dtype) @ wo

def rotary(x, pos):
    half = x.shape[-1] // 2
    inv = ROPE_BASE ** (-jnp.arange(half, dtype=jnp.float32) / half)
    ang = pos[:, None] * inv[None, :]
    cos, sin = jnp.cos(ang), jnp.sin(ang)
    x1, x2 = x[..., :half], x[..., half:]
    return jnp.concatenate([x1 * cos - x2 * sin, x1 * sin + x2 * cos], axis=-1)

def retention_mixer(h, wq, wk, wv, wg, gn, wo):
    B, S, _ = h.shape
    H, dk, dv, C = RET_HEADS, RET_QK_DIM, RET_V_DIM, RET_CHUNK
    pos = jnp.arange(S, dtype=jnp.float32)
    q = (h @ wq).reshape(B, S, H, dk).transpose(0, 2, 1, 3).astype(jnp.float32)
    k = (h @ wk).reshape(B, S, H, dk).transpose(0, 2, 1, 3).astype(jnp.float32)
    v = (h @ wv).reshape(B, S, H, dv).transpose(0, 2, 1, 3).astype(jnp.float32)
    q = rotary(q, pos)
    k = rotary(k, pos) * (dk ** -0.5)

    log_gamma = jnp.log1p(-jnp.exp2(-5.0 - jnp.arange(H, dtype=jnp.float32)))
    idx = jnp.arange(C, dtype=jnp.float32)
    diff = idx[:, None] - idx[None, :]
    decay_in = jnp.where(diff >= 0,
                         jnp.exp(log_gamma[:, None, None] * jnp.maximum(diff, 0.0)), 0.0)
    q_decay = jnp.exp(log_gamma[:, None] * (idx + 1.0))[:, :, None]
    k_decay = jnp.exp(log_gamma[:, None] * (C - 1.0 - idx))[:, :, None]
    chunk_decay = jnp.exp(log_gamma * C)[:, None, None]

    nc = S // C
    qc = q.reshape(B, H, nc, C, dk).transpose(2, 0, 1, 3, 4)
    kc = k.reshape(B, H, nc, C, dk).transpose(2, 0, 1, 3, 4)
    vc = v.reshape(B, H, nc, C, dv).transpose(2, 0, 1, 3, 4)

    def step(state, xs):
        qi, ki, vi = xs
        inner = jnp.einsum('bhid,bhjd->bhij', qi, ki) * decay_in
        o = (jnp.einsum('bhij,bhje->bhie', inner, vi)
             + jnp.einsum('bhid,bhde->bhie', qi * q_decay, state))
        state = chunk_decay * state + jnp.einsum('bhjd,bhje->bhde', ki * k_decay, vi)
        return state, o

    state0 = jnp.zeros((B, H, dk, dv), jnp.float32)
    _, o = lax.scan(step, state0, (qc, kc, vc))
    o = o.transpose(1, 0, 3, 2, 4).reshape(B, S, H, dv)
    o = o * lax.rsqrt(jnp.mean(jnp.square(o), axis=-1, keepdims=True) + RMS_EPS)
    o = o.reshape(B, S, H * dv) * gn.astype(jnp.float32)
    gate = jax.nn.silu((h @ wg).astype(jnp.float32))
    return (gate * o).astype(h.dtype) @ wo

def sqrelu_mlp(h, w_up, w_down):
    return jnp.square(jax.nn.relu(h @ w_up)) @ w_down

def setup_inputs(seed: int = 0) -> dict:
    key = jax.random.key(seed)
    ks = jax.random.split(key, 24)
    D = D_MODEL

    def w(k, shape, fan_in):
        return jax.random.normal(k, shape, jnp.float32) * (fan_in ** -0.5)

    def gain(k, shape):
        return 1.0 + 0.05 * jax.random.normal(k, shape, jnp.float32)

    fd = FOX_HEADS * FOX_HEAD_DIM
    rk = RET_HEADS * RET_QK_DIM
    rv = RET_HEADS * RET_V_DIM
    return {
        "x": jax.random.normal(ks[0], (BATCH, SEQ, D), jnp.float32),
        "fox_norm": gain(ks[1], (N_FOX, D)),
        "fox_wq": w(ks[2], (N_FOX, D, fd), D),
        "fox_wk": w(ks[3], (N_FOX, D, fd), D),
        "fox_wv": w(ks[4], (N_FOX, D, fd), D),
        "fox_wf": w(ks[5], (N_FOX, D, FOX_HEADS), D),
        "fox_bf": jax.random.uniform(ks[6], (N_FOX, FOX_HEADS), jnp.float32, 1.0, 5.0),
        "fox_wo": w(ks[7], (N_FOX, fd, D), fd),
        "ret_norm": gain(ks[8], (N_RET, D)),
        "ret_wq": w(ks[9], (N_RET, D, rk), D),
        "ret_wk": w(ks[10], (N_RET, D, rk), D),
        "ret_wv": w(ks[11], (N_RET, D, rv), D),
        "ret_wg": w(ks[12], (N_RET, D, rv), D),
        "ret_gn": gain(ks[13], (N_RET, rv)),
        "ret_wo": w(ks[14], (N_RET, rv, D), rv),
        "mlp_norm": gain(ks[15], (DEPTH, D)),
        "mlp_up": w(ks[16], (DEPTH, D, D_FF), D),
        "mlp_down": w(ks[17], (DEPTH, D_FF, D), D_FF),
        "final_norm": gain(ks[18], (D,)),
    }

def reference(x, fox_norm, fox_wq, fox_wk, fox_wv, fox_wf, fox_bf, fox_wo,
              ret_norm, ret_wq, ret_wk, ret_wv, ret_wg, ret_gn, ret_wo,
              mlp_norm, mlp_up, mlp_down, final_norm):
    h = x
    for layer in range(DEPTH):
        j = layer // N_MIXERS
        if layer % N_MIXERS == 0:
            h = h + fox_mixer(rmsnorm(h, fox_norm[j]), fox_wq[j], fox_wk[j], fox_wv[j],
                              fox_wf[j], fox_bf[j], fox_wo[j])
        else:
            h = h + retention_mixer(rmsnorm(h, ret_norm[j]), ret_wq[j], ret_wk[j], ret_wv[j],
                                    ret_wg[j], ret_gn[j], ret_wo[j])
        h = h + sqrelu_mlp(rmsnorm(h, mlp_norm[layer]), mlp_up[layer], mlp_down[layer])
    return rmsnorm(h, final_norm)


_drawn_inputs = setup_inputs


def setup_inputs(seed=0):
    import zlib

    import numpy as np

    out = dict(_drawn_inputs(seed))
    spreads = {}
    factors = {'ret_gn': 3.155}
    for name, (base, spread) in spreads.items():
        noise = np.random.default_rng([zlib.crc32(name.encode()), seed]).standard_normal(out[name].shape)
        drawn = base * np.exp(spread * noise) if base else spread * noise
        out[name] = __import__('jax').numpy.asarray(drawn.astype(out[name].dtype))
    for name, factor in factors.items():
        out[name] = (out[name] * factor).astype(out[name].dtype)
    return out
```

```python
from contextlib import ExitStack

import concourse.bass as bass
from concourse import mybir
from concourse.alu_op_type import AluOpType as ALU

F32 = mybir.dt.float32
F32R = mybir.dt.float32r
ACT = mybir.ActivationFunctionType
AX_X = mybir.AxisListType.X

P = 128
D = 2048
S = 256
TOKS = S // P
NB = 512
KT = D // P
PER_SLOT = 2
SLOTS = KT // PER_SLOT
SW = PER_SLOT * NB
RAW = 4
QUADS = D // NB
FOX_HEADS, FOX_DIM = 16, 128
HPG = NB // FOX_DIM
GROUPS = FOX_HEADS // HPG
RET_HEADS, RET_QK, RET_V = 8, 256, 512
RET_HALF = RET_HEADS // 2
D_FF = 8192
SUPER = D_FF // D
EPS = 1e-6
MASKED = -3e38
FOX_BLOCKS = GROUPS * 3 + QUADS
MLP_BLOCKS = SUPER * 2 * QUADS
RET_BLOCKS = 2 * (RET_HALF * 3 + QUADS)
BLOCKS = FOX_BLOCKS + RET_BLOCKS + 2 * MLP_BLOCKS

C_ID, C_TRI, C_ONE, C_MASK = 0, P, 2 * P, 3 * P
C_COS = C_MASK + 3 * P
C_SIN = C_COS + TOKS * P
C_END = C_SIN + TOKS * P


class Tally:

    def __init__(self, *names):
        self.base = dict.fromkeys(names, 0)
        self.off = dict.fromkeys(names, 0)

    def __call__(self, name, more=0):
        base, off = self.base[name], self.off[name] + more
        return off if isinstance(base, int) and base == 0 else base + off

    def up(self, name, by=1):
        self.off[name] += by

    def loop(self, eng, n, body, **per_round):
        before, start = dict(self.base), dict(self.off)
        with eng.Fori(0, n) as i:
            for k, d in per_round.items():
                self.base[k] = i * d + before[k]
            body(i)
        moved = {k: self.off[k] - start[k] for k in self.off if self.off[k] != start[k]}
        assert moved == per_round, (moved, per_round)
        for k, d in per_round.items():
            self.base[k] = before[k]
            self.off[k] = start[k] + n * d


def build_trunk(nc, x, w_stream, gains, gn, wf, bf, consts, decay, out):
    with ExitStack() as ctx:
        def sb(name, cols, dt=F32, parts=P):
            return ctx.enter_context(nc.sbuf_tensor(name, [parts, cols], dt))

        def sem(name):
            return ctx.enter_context(nc.semaphore(name))

        def pair(name):
            return [sem(f"{name}{t}") for t in range(TOKS)]

        h = sb("h", TOKS * D)
        xT_hi, xT_lo = sb("xT_hi", TOKS * D, F32R), sb("xT_lo", TOKS * D, F32R)
        aT_hi, aT_lo = sb("aT_hi", TOKS * D, F32R), sb("aT_lo", TOKS * D, F32R)
        raw = sb("raw", RAW * SW)
        w_hi, w_lo = sb("w_hi", SLOTS * SW, F32R), sb("w_lo", SLOTS * SW, F32R)
        const = sb("const", C_END)
        gain = sb("gain", D)
        stage = [sb(f"stage{t}", NB) for t in range(TOKS)]
        evac = [sb(f"evac{t}", NB) for t in range(TOKS)]
        wf_hi, wf_lo = sb("wf_hi", KT * FOX_HEADS, F32R), sb("wf_lo", KT * FOX_HEADS, F32R)
        stat = sb("stat", 160)
        scratch = sb("scratch", 21 * 256)
        negc = sb("negc", S, F32, HPG)

        ident = const[:, C_ID:C_ID + P]
        tri = const[:, C_TRI:C_TRI + P]
        ones = const[:, C_ONE:C_ONE + P]
        mask = const[:, C_MASK:C_MASK + 3 * P]

        at = [0]

        def cols(n):
            at[0] += n
            return stat[:, at[0] - n:at[0]]

        sumsq = cols(TOKS * QUADS)
        mean_sq = cols(TOKS)
        mean_eps = cols(TOKS)
        inv_ms = cols(TOKS)
        root = cols(TOKS)
        rstd = cols(TOKS)
        rstd_q = cols(TOKS)
        row_max = cols(2 * TOKS)
        row_sum = cols(2 * TOKS)
        row_inv = cols(2 * TOKS)
        gsum, gmean, groot, grstd = cols(TOKS), cols(TOKS), cols(TOKS), cols(TOKS)
        log_f_group = cols(TOKS * HPG)
        c_group = cols(TOKS * HPG)
        assert at[0] <= 160

        def cut(start, n):
            return scratch[:, start:start + n]

        kT, qT = cut(0, HPG * S), cut(1024, HPG * S)
        v_fox = [cut(2048 + t * NB, NB) for t in range(TOKS)]
        probs = [cut(3072 + b * 384, 384) for b in range(2)]
        pT = cut(3840, HPG * 384)
        wf_raw = cut(0, KT * FOX_HEADS)
        gate_z, gate_a, gate_e, gate_l, gate_m = (cut(3840 + 32 * n, 32) for n in range(5))
        log_f = sb("log_f", TOKS * FOX_HEADS)
        bias_f = cut(3840 + 32 * 6, FOX_HEADS)
        qkT = cut(0, 4 * S)
        v_ret = [cut(1024 + t * NB, NB) for t in range(TOKS)]
        gate_r = [cut(2048 + t * NB, NB) for t in range(TOKS)]
        inner = cut(3072, 384)
        decay_t = cut(3456, 384)
        gn_t = cut(3840, RET_V)
        rot = cut(4352, 4 * S)

        def bank(name):
            return ctx.enter_context(nc.psum_tensor(name, [P, NB], F32))

        acc = [bank(f"acc{t}") for t in range(TOKS)]
        tr = [bank(f"tr{t}") for t in range(TOKS)]
        sc = [bank(f"sc{b}") for b in range(2)]
        mix = [bank(f"mix{b}") for b in range(2)]

        raw_in = [sem(f"raw_in{r}") for r in range(RAW)]
        hi_made = sem("hi_made")
        lo_made = sem("lo_made")
        w_used = sem("w_used")
        acc_done = pair("acc_done")
        acc_out = pair("acc_out")
        staged = pair("staged")
        tr_done = pair("tr_done")
        tr_hi = pair("tr_hi")
        tr_out = pair("tr_out")
        x_in = pair("x_in")
        gain0_in, gain_in = sem("gain0_in"), sem("gain_in")
        const_in = sem("const_in")
        wf_in, bias_in = sem("wf_in"), sem("bias_in")
        wf_hi_made, wf_made = sem("wf_hi_made"), sem("wf_made")
        squared = sem("squared")
        mean_made = sem("mean_made")
        root_made = sem("root_made")
        norm_made = sem("norm_made")
        dve_step = sem("dve_step")
        gate_done, gate_zed, gate_exp, gate_ln = (sem(n) for n in ("gate_done", "gate_zed", "gate_exp", "gate_ln"))
        cum_src, cum_done, cum_out = sem("cum_src"), sem("cum_done"), sem("cum_out")
        score_done = sem("score_done")
        score_out = sem("score_out")
        exp_made = sem("exp_made")
        probs_made = sem("probs_made")
        pT_done, pT_out = sem("pT_done"), sem("pT_out")
        table_in = sem("table_in")
        inner_made = sem("inner_made")
        mixed = sem("mixed")
        gsq, gmean_made, groot_made, grstd_made = (sem(n) for n in (
            "gsq", "gmean_made", "groot_made", "grstd_made"))
        gated = pair("gated")
        out_ready = sem("out_ready")
        stored = sem("stored")

        block = ctx.enter_context(nc.Block())

        def wait(eng, s, value):
            if not (isinstance(value, int) and value <= 0):
                eng.wait_ge(s, value)

        def slot_cols(s, kk):
            return slice(s * SW + kk * NB, s * SW + (kk + 1) * NB)

        @block.sync
        def _(sp):
            for t in range(TOKS):
                sp.dma_start(h[:, t * D:(t + 1) * D], x[t * P:(t + 1) * P, :]).then_inc(x_in[t], 16)
                if t == 0:
                    sp.dma_start(gain[:, :], gains[0]).then_inc(gain0_in, 16)
                    sp.dma_start(const[:, :], consts).then_inc(const_in, 16)
            sp.dma_start(wf_raw, wf).then_inc(wf_in, 16)
            for s in range(SLOTS):
                if s >= RAW:
                    sp.wait_ge(lo_made, s - RAW + 1)
                sp.dma_start(raw[:, s % RAW * SW:(s % RAW + 1) * SW], w_stream[0, s]).then_inc(raw_in[s % RAW], 16)
            with sp.Fori(1, BLOCKS) as b:
                for s in range(SLOTS):
                    sp.wait_ge(lo_made, b * SLOTS + (s - RAW + 1))
                    sp.dma_start(raw[:, s % RAW * SW:(s % RAW + 1) * SW],
                                 w_stream[bass.ds(b, 1), s].rearrange("o p n -> (o p) n")
                                 ).then_inc(raw_in[s % RAW], 16)
            for t in range(TOKS):
                sp.wait_ge(out_ready, t + 1)
                sp.dma_start(out[t * P:(t + 1) * P, :], h[:, t * D:(t + 1) * D]).then_inc(stored, 16)
            sp.wait_ge(stored, 16 * TOKS)

        @block.gpsimd
        def _(pool):
            pool.dma_start(bias_f, bf).then_inc(bias_in, 16)
            fox_staged = QUADS + QUADS
            mlp_staged = SUPER * QUADS + QUADS
            ret_staged = RET_HEADS * 2 + QUADS
            last_use = [QUADS, fox_staged, fox_staged + mlp_staged, fox_staged + mlp_staged + ret_staged]

            def load_gain(n):
                for t in range(TOKS):
                    pool.wait_ge(staged[t], last_use[n - 1])
                pool.dma_start(gain[:, :], gains[n]).then_inc(gain_in, 16)

            load_gain(1)
            load_gain(2)
            load_gain(3)
            T = Tally("head", "block")
            T.up("block", FOX_BLOCKS + MLP_BLOCKS)

            def head(i):
                wait(pool, inner_made, T("head"))
                wait(pool, gated[1], T("head"))
                pool.dma_start(decay_t, decay[bass.ds(T("head"), 1)].rearrange("o p n -> (o p) n")
                               ).then_inc(table_in, 16)
                pool.dma_start(gn_t, gn[bass.ds(T("head"), 1)].rearrange("o p n -> (o p) n")
                               ).then_inc(table_in, 16)
                pool.wait_ge(table_in, T("head") * 32 + 32)
                for t in range(TOKS):
                    pool.wait_ge(acc_out[t], T("block") + 3)
                    pool.tensor_tensor(gate_r[t], gate_r[t], gn_t, ALU.mult).then_inc(gated[t], 1)
                T.up("head")
                T.up("block", 3)

            head(0)
            T.loop(pool, RET_HALF - 1, head, head=1, block=3)
            T.up("block", QUADS)
            T.loop(pool, RET_HALF, head, head=1, block=3)
            load_gain(4)

        @block.tensor
        def _(pe):
            T = Tally("block", "tr0", "tr1", "staged0", "staged1", "group", "ret_head")

            def product(lhs, tok, first, last):
                hi_t, lo_t = lhs
                for s in range(first, last):
                    if s == 0:
                        wait(pe, acc_out[tok], T("block"))
                        wait(pe, tr_out[tok], T(f"tr{tok}"))
                    if tok == 0:
                        pe.wait_ge(lo_made, T("block") * SLOTS + (s + 1))
                    for kk in range(PER_SLOT):
                        kt = s * PER_SLOT + kk
                        x_cols = slice(tok * D + kt * P, tok * D + (kt + 1) * P)
                        w_cols = slot_cols(s, kk)
                        pe.matmul(acc[tok][:, :], hi_t[:, x_cols], w_hi[:, w_cols], start=(kt == 0), stop=False)
                        pe.matmul(acc[tok][:, :], hi_t[:, x_cols], w_lo[:, w_cols], start=False, stop=False)
                        m = pe.matmul(acc[tok][:, :], lo_t[:, x_cols], w_hi[:, w_cols], start=False,
                                      stop=(kt == KT - 1))
                    if s == SLOTS - 1:
                        m.then_inc(acc_done[tok], 1)
                    elif tok == TOKS - 1:
                        m.then_inc(w_used, 1)

            def batch(tok, by_act=False, blocks_ago=0):
                if by_act:
                    pe.wait_ge(acc_out[tok], T("block", 1 - blocks_ago))
                else:
                    T.up(f"staged{tok}")
                    pe.wait_ge(staged[tok], T(f"staged{tok}"))
                wait(pe, tr_out[tok], T(f"tr{tok}"))
                for j in range(NB // P):
                    m = pe.transpose(tr[tok][:, j * P:(j + 1) * P], stage[tok][:, j * P:(j + 1) * P], ident)
                m.then_inc(tr_done[tok], 1)
                T.up(f"tr{tok}")

            def run_block(lhs, mid0=None, mid1=None):
                product(lhs, 0, 0, 4)
                if mid0:
                    mid0()
                product(lhs, 0, 4, 8)
                product(lhs, 1, 0, 4)
                if mid1:
                    mid1()
                product(lhs, 1, 4, 8)
                T.up("block")

            xT, aT = (xT_hi, xT_lo), (aT_hi, aT_lo)
            pending = lambda: batch(1)
            own = lambda: batch(0)

            pe.wait_ge(const_in, 16)
            for n in range(QUADS):
                batch(0)
                batch(1)

            def forget_gate():
                pe.wait_ge(wf_made, 1)
                for tok in range(TOKS):
                    pe.wait_ge(tr_out[tok], T(f"tr{tok}"))
                    z = sc[0][:, tok * FOX_HEADS:(tok + 1) * FOX_HEADS]
                    for kt in range(KT):
                        x_cols = slice(tok * D + kt * P, tok * D + (kt + 1) * P)
                        f_cols = slice(kt * FOX_HEADS, (kt + 1) * FOX_HEADS)
                        pe.matmul(z, xT_hi[:, x_cols], wf_hi[:, f_cols], start=(kt == 0), stop=False)
                        pe.matmul(z, xT_hi[:, x_cols], wf_lo[:, f_cols], start=False, stop=False)
                        m = pe.matmul(z, xT_lo[:, x_cols], wf_hi[:, f_cols], start=False, stop=(kt == KT - 1))
                m.then_inc(gate_done, 1)

            def cumulate():
                pe.wait_ge(cum_src, T("group") + 1)
                f = [log_f_group[:, t * HPG:(t + 1) * HPG] for t in range(TOKS)]
                c = sc[0]
                pe.matmul(c[:, 0:HPG], tri, f[0], start=True, stop=True)
                pe.matmul(c[:, HPG:2 * HPG], ones, f[0], start=True, stop=False)
                pe.matmul(c[:, HPG:2 * HPG], tri, f[1], start=False, stop=True)
                pe.matmul(c[0:HPG, P:2 * P], f[0], tri, start=True, stop=True)
                pe.matmul(c[0:HPG, 2 * P:3 * P], f[0], ones, start=True, stop=False)
                pe.matmul(c[0:HPG, 2 * P:3 * P], f[1], tri, start=False, stop=True).then_inc(cum_done, 1)

            def scores(j):
                b = sc[j % 2]
                if j == 0:
                    pe.wait_ge(cum_out, T("group") + 1)
                    for t in range(TOKS):
                        pe.wait_ge(tr_out[t], T(f"tr{t}"))
                if j >= 2:
                    pe.wait_ge(score_out, T("group") * HPG + (j - 1))
                pick = ident[0:HPG, j:j + 1].broadcast_to([HPG, P])
                q, k = qT[:, j * S:(j + 1) * S], kT[:, j * S:(j + 1) * S]
                pe.matmul(b[:, 0:P], q[:, 0:P], k[:, 0:P], start=True, stop=False)
                pe.matmul(b[:, 0:P], pick, negc[:, 0:P], start=False, stop=True)
                pe.matmul(b[:, P:3 * P], q[:, P:S], k[:, 0:S], start=True, stop=False)
                pe.matmul(b[:, P:3 * P], pick, negc[:, 0:S], start=False, stop=True).then_inc(score_done, 1)

            def transpose_probs(j):
                b = mix[j % 2]
                pe.wait_ge(probs_made, T("group") * HPG + (j + 1))
                if j >= 2:
                    pe.wait_ge(pT_out, T("group") * HPG + (j - 1))
                for part in range(3):
                    m = pe.transpose(b[:, part * P:(part + 1) * P], probs[j % 2][:, part * P:(part + 1) * P], ident)
                m.then_inc(pT_done, 1)

            def mix_values(tok, blocks_ago):
                pe.wait_ge(acc_out[tok], T("block", 1 - blocks_ago))
                pe.wait_ge(pT_out, T("group") * HPG)
                wait(pe, tr_out[tok], T(f"tr{tok}"))
                for j in range(HPG):
                    v_cols = slice(j * FOX_DIM, (j + 1) * FOX_DIM)
                    o = tr[tok][:, j * P:(j + 1) * P]
                    pj = pT[:, j * 384:(j + 1) * 384]
                    if tok == 0:
                        m = pe.matmul(o, v_fox[0][:, v_cols], pj[:, 0:P], start=True, stop=True)
                    else:
                        pe.matmul(o, v_fox[0][:, v_cols], pj[:, P:2 * P], start=True, stop=False)
                        m = pe.matmul(o, v_fox[1][:, v_cols], pj[:, 2 * P:3 * P], start=False, stop=True)
                m.then_inc(tr_done[tok], 1)
                T.up(f"tr{tok}")

            def k_own():
                batch(0, by_act=True)

            def k_pending():
                batch(1, by_act=True, blocks_ago=1)

            def q_own_and_cum():
                k_own()
                cumulate()

            def v_block():
                product(xT, 0, 0, 2)
                k_pending()
                product(xT, 0, 2, 4)
                scores(0)
                product(xT, 0, 4, 6)
                scores(1)
                product(xT, 0, 6, 8)
                transpose_probs(0)
                scores(2)
                product(xT, 1, 0, 2)
                transpose_probs(1)
                scores(3)
                product(xT, 1, 2, 4)
                transpose_probs(2)
                product(xT, 1, 4, 6)
                transpose_probs(3)
                T.up("group")
                product(xT, 1, 6, 7)
                mix_values(0, 0)
                product(xT, 1, 7, 8)
                T.up("block")

            def mix_pending():
                mix_values(1, 1)

            forget_gate()
            run_block(xT, None, k_own)

            def group_but_k(i):
                run_block(xT, k_pending, q_own_and_cum)
                v_block()

            def group_and_k(i):
                group_but_k(i)
                run_block(xT, mix_pending, k_own)

            T.loop(pe, GROUPS - 1, group_and_k, block=3, tr0=3, tr1=3, group=1)
            group_but_k(None)
            run_block(aT, mix_pending, own)
            T.loop(pe, QUADS - 1, lambda i: run_block(aT, pending, own),
                   block=1, tr0=1, tr1=1, staged0=1, staged1=1)

            def mlp(last):
                run_block(xT, pending, own)

                def ups(i):
                    T.loop(pe, QUADS - 1, lambda i: run_block(xT, pending, own),
                           block=1, tr0=1, tr1=1, staged0=1, staged1=1)

                def chunk(i):
                    ups(i)
                    run_block(aT, pending)
                    T.loop(pe, QUADS - 1, lambda i: run_block(aT), block=1)
                    run_block(xT, None, own)

                T.loop(pe, SUPER - 1, chunk, block=2 * QUADS, tr0=QUADS, tr1=QUADS, staged0=QUADS, staged1=QUADS)
                ups(None)
                if last:
                    run_block(aT, pending)
                    T.loop(pe, QUADS - 1, lambda i: run_block(aT), block=1)
                else:
                    run_block(aT, pending, own)
                    T.loop(pe, QUADS - 1, lambda i: run_block(aT, pending, own),
                           block=1, tr0=1, tr1=1, staged0=1, staged1=1)

            mlp(last=False)

            def ret_scores():
                for t in range(TOKS):
                    pe.wait_ge(tr_out[t], T(f"tr{t}"))
                q = [qkT[:, dd * S:(dd + 1) * S] for dd in range(2)]
                k = [qkT[:, (2 + dd) * S:(3 + dd) * S] for dd in range(2)]
                for dd in range(2):
                    pe.matmul(sc[0][:, 0:S], k[dd][:, 0:P], q[dd], start=(dd == 0), stop=(dd == 1))
                for dd in range(2):
                    m = pe.matmul(sc[0][:, S:S + P], k[dd][:, P:S], q[dd][:, P:S], start=(dd == 0), stop=(dd == 1))
                m.then_inc(score_done, 1)
                T.up("ret_head")

            def ret_mix():
                pe.wait_ge(inner_made, T("ret_head"))
                for t in range(TOKS):
                    pe.wait_ge(acc_out[t], T("block"))
                pe.matmul(mix[0][:, :], inner[:, 0:P], v_ret[0], start=True, stop=True)
                pe.matmul(mix[1][:, :], inner[:, P:2 * P], v_ret[0], start=True, stop=False)
                pe.matmul(mix[1][:, :], inner[:, 2 * P:3 * P], v_ret[1], start=False, stop=True).then_inc(mixed, 1)

            def ret_v_and_gate(i):
                run_block(xT, pending, ret_scores)
                run_block(xT, ret_mix, own)

            def ret_head(i):
                ret_v_and_gate(i)
                run_block(xT, pending, own)

            def ret_half(first_pending, last):
                run_block(xT, first_pending, own)
                T.loop(pe, RET_HALF - 1, ret_head, block=3, tr0=2, tr1=2, staged0=2, staged1=2, ret_head=1)
                ret_v_and_gate(None)
                if last:
                    T.loop(pe, QUADS, lambda i: run_block(aT, pending, own),
                           block=1, tr0=1, tr1=1, staged0=1, staged1=1)
                else:
                    run_block(aT, pending)
                    T.loop(pe, QUADS - 1, lambda i: run_block(aT), block=1)

            ret_half(pending, last=False)
            ret_half(None, last=True)
            mlp(last=True)

        @block.scalar
        def _(act):
            T = Tally("block", "tr0", "tr1", "squared", "group", "ret_head", "norm")

            def split(first, last, block0=False):
                for s in range(first, last):
                    use = s // RAW + 1
                    if block0:
                        act.wait_ge(raw_in[s % RAW], 16 * use)
                    else:
                        act.wait_ge(raw_in[s % RAW], T("block") * (16 * SLOTS // RAW) + 16 * (SLOTS // RAW + use))
                        if s == SLOTS - 1:
                            act.wait_ge(acc_done[1], T("block", 1))
                        else:
                            act.wait_ge(w_used, T("block") * (SLOTS - 1) + (s + 1))
                    act.activation(w_hi[:, s * SW:(s + 1) * SW], raw[:, s % RAW * SW:(s % RAW + 1) * SW],
                                   ACT.Copy).then_inc(hi_made, 1)

            def batch_hi(tok, dst, quad):
                act.wait_ge(tr_done[tok], T(f"tr{tok}", 1))
                act.activation(dst[:, bass.ds(quad * NB + tok * D, NB)], tr[tok][:, :], ACT.Copy).then_inc(tr_hi[tok], 1)
                T.up(f"tr{tok}")

            def batch_qk(tok, dst):
                act.wait_ge(tr_done[tok], T(f"tr{tok}", 1))
                act.activation(dst.rearrange("p (j s) -> p j s", j=4)[:, :, tok * P:(tok + 1) * P],
                               tr[tok][:, :].rearrange("p (j s) -> p j s", j=4), ACT.Copy).then_inc(tr_out[tok], 1)
                T.up(f"tr{tok}")

            def acc_to(tok, dst, func, scale):
                act.wait_ge(acc_done[tok], T("block", 1))
                act.activation(dst, acc[tok][:, :], func, scale=scale).then_inc(acc_out[tok], 1)

            def square(tok, quad):
                wait(act, squared, T("squared"))
                act.activation(evac[tok][:, :], h[:, bass.ds(quad * NB + tok * D, NB)], ACT.Square,
                               accum_out=sumsq[:, bass.ds(quad + tok * QUADS, 1)]).then_inc(squared, 1)
                T.up("squared")

            def roots():
                T.up("norm")
                act.wait_ge(mean_made, T("norm"))
                act.activation(root, mean_eps, ACT.Sqrt).then_inc(root_made, 1)

            def factor(t, col):
                return col[:, t:t + 1]

            act.wait_ge(wf_in, 16)
            act.activation(wf_hi[:, :], wf_raw, ACT.Copy).then_inc(wf_hi_made, 1)
            for n in range(QUADS):
                for tok in range(TOKS):
                    if n == 0:
                        act.wait_ge(x_in[tok], 16)
                    square(tok, n)
                    batch_hi(tok, xT_hi, n)
                if n:
                    split(2 * n - 2, 2 * n, block0=True)
            split(SLOTS - 2, SLOTS, block0=True)
            roots()

            act.wait_ge(gate_zed, 1)
            act.activation(gate_e, gate_a, ACT.Exp, scale=-1.0).then_inc(gate_exp, 1)
            act.wait_ge(gate_exp, 1)
            act.activation(gate_l, gate_e, ACT.Ln, bias=1.0).then_inc(gate_ln, 1)

            def proj(scale, dst):
                acc_to(0, stage[0][:, :], ACT.Copy, factor(0, scale))
                split(0, 2)
                batch_qk(0, dst)
                split(2, 7)
                acc_to(1, stage[1][:, :], ACT.Copy, factor(1, scale))
                split(7, 8)
                T.up("block")
                batch_qk(1, dst)

            def exponentials(j):
                act.wait_ge(score_out, T("group") * HPG + (j + 1))
                b, p = 2 * (j % 2), probs[j % 2]
                act.activation(p[:, 0:P], p[:, 0:P], ACT.Exp, bias=row_max[:, b:b + 1],
                               accum_out=row_sum[:, b:b + 1])
                act.activation(p[:, P:3 * P], p[:, P:3 * P], ACT.Exp, bias=row_max[:, b + 1:b + 2],
                               accum_out=row_sum[:, b + 1:b + 2]).then_inc(exp_made, 1)

            def probs_T(j):
                act.wait_ge(pT_done, T("group") * HPG + (j + 1))
                act.activation(pT[:, j * 384:(j + 1) * 384], mix[j % 2][:, 0:384], ACT.Copy).then_inc(pT_out, 1)

            def group(g):
                proj(rstd, kT)
                proj(rstd_q, qT)
                exponentials(0)
                exponentials(1)
                acc_to(0, v_fox[0], ACT.Copy, factor(0, rstd))
                exponentials(2)
                probs_T(0)
                exponentials(3)
                probs_T(1)
                split(0, 2)
                probs_T(2)
                split(2, 4)
                probs_T(3)
                split(4, 6)
                batch_hi(0, aT_hi, g)
                split(6, 7)
                acc_to(1, v_fox[1], ACT.Copy, factor(1, rstd))
                split(7, 8)
                T.up("block")
                T.up("group")
                batch_hi(1, aT_hi, g)

            act.wait_ge(norm_made, 1)
            T.loop(act, GROUPS, group, block=3, tr0=3, tr1=3, group=1)

            def add_block(n, normed=False, batches=False, feeds=True):
                if normed:
                    act.wait_ge(acc_out[0], T("block", 1))
                    square(0, n)
                if feeds:
                    split(0, 2)
                if batches:
                    batch_hi(0, xT_hi, n)
                if feeds:
                    split(2, 7)
                if normed:
                    act.wait_ge(acc_out[1], T("block", 1))
                    square(1, n)
                if feeds:
                    split(7, 8)
                T.up("block")
                if batches:
                    batch_hi(1, xT_hi, n)

            def adds(normed):
                if normed:
                    T.loop(act, QUADS, lambda n: add_block(n, normed=True, batches=True),
                           block=1, tr0=1, tr1=1, squared=2)
                else:
                    T.loop(act, QUADS, add_block, block=1)

            def up_block(u):
                acc_to(0, evac[0][:, :], ACT.Relu, 1.0)
                split(0, 2)
                batch_hi(0, aT_hi, u)
                split(2, 7)
                acc_to(1, evac[1][:, :], ACT.Relu, 1.0)
                split(7, 8)
                T.up("block")
                batch_hi(1, aT_hi, u)

            def mlp(last):
                def ups():
                    T.loop(act, QUADS, up_block, block=1, tr0=1, tr1=1)

                def chunk(i):
                    ups()
                    adds(normed=False)

                act.wait_ge(squared, T("squared"))
                T.up("norm")
                T.loop(act, SUPER - 1, chunk, block=2 * QUADS, tr0=QUADS, tr1=QUADS)
                ups()
                if last:
                    T.loop(act, QUADS - 1, lambda n: add_block(n, normed=True), block=1, squared=2)
                    add_block(QUADS - 1, normed=True, feeds=False)
                else:
                    adds(normed=True)

            adds(normed=True)
            mlp(last=False)
            roots()
            act.wait_ge(norm_made, 2)

            def ret_head(i):
                acc_to(0, evac[0][:, :], ACT.Copy, factor(0, rstd))
                split(0, 2)
                batch_qk(0, qkT)
                split(2, 7)
                acc_to(1, evac[1][:, :], ACT.Copy, factor(1, rstd))
                split(7, 8)
                T.up("block")
                batch_qk(1, qkT)
                acc_to(0, v_ret[0], ACT.Copy, factor(0, rstd))
                split(0, 7)
                acc_to(1, v_ret[1], ACT.Copy, factor(1, rstd))
                split(7, 8)
                T.up("block")
                act.wait_ge(mixed, T("ret_head", 1))
                for t in range(TOKS):
                    act.activation(gate_r[t], mix[t][:, :], ACT.Square, accum_out=gsum[:, t:t + 1]).then_inc(gsq, 1)
                act.wait_ge(gmean_made, T("ret_head", 1))
                act.activation(groot, gmean, ACT.Sqrt).then_inc(groot_made, 1)
                acc_to(0, gate_r[0], ACT.Silu, factor(0, rstd))
                split(0, 2)
                batch_hi(0, aT_hi, i)
                split(2, 7)
                acc_to(1, gate_r[1], ACT.Silu, factor(1, rstd))
                split(7, 8)
                T.up("block")
                batch_hi(1, aT_hi, i)
                T.up("ret_head")

            for half in range(2):
                T.loop(act, RET_HALF, ret_head, block=3, tr0=2, tr1=2, ret_head=1)
                adds(normed=(half == 1))
            mlp(last=True)
            roots()

        @block.vector
        def _(dve):
            T = Tally("block", "hi0", "hi1", "step", "norm", "mixer_norm", "group", "ret_head")

            def step(ins):
                ins.then_inc(dve_step, 1)
                T.up("step")
                dve.wait_ge(dve_step, T("step"))

            def split(first, last, block0=False):
                for s in range(first, last):
                    dve.wait_ge(hi_made, s + 1 if block0 else T("block") * SLOTS + (SLOTS + s + 1))
                    c = slice(s * SW, (s + 1) * SW)
                    dve.tensor_tensor(w_lo[:, c], raw[:, s % RAW * SW:(s % RAW + 1) * SW],
                                      w_hi[:, c].bitcast(F32), ALU.subtract).then_inc(lo_made, 1)

            def batch_lo(tok, dst_hi, dst_lo, quad):
                T.up(f"hi{tok}")
                dve.wait_ge(tr_hi[tok], T(f"hi{tok}"))
                c = bass.ds(quad * NB + tok * D, NB)
                dve.tensor_tensor(dst_lo[:, c], tr[tok][:, :], dst_hi[:, c].bitcast(F32),
                                  ALU.subtract).then_inc(tr_out[tok], 1)

            def gained(tok, quad):
                dve.tensor_tensor(stage[tok][:, :], h[:, bass.ds(quad * NB + tok * D, NB)],
                                  gain[:, bass.ds(quad * NB, NB)], ALU.mult).then_inc(staged[tok], 1)

            def mean_squares():
                T.up("norm")
                dve.wait_ge(squared, T("norm") * TOKS * QUADS)
                step(dve.tensor_reduce(mean_sq, sumsq.rearrange("p (t n) -> p t n", t=TOKS), AX_X, ALU.add))
                dve.tensor_scalar(mean_eps, mean_sq, 1.0 / D, EPS, ALU.mult, ALU.add).then_inc(mean_made, 1)
                dve.wait_ge(mean_made, T("norm"))

            def norm_for_mixer():
                mean_squares()
                T.up("mixer_norm")
                dve.wait_ge(root_made, T("mixer_norm"))
                step(dve.reciprocal(rstd, root))
                dve.tensor_scalar(rstd_q, rstd, FOX_DIM ** -0.5, None, ALU.mult).then_inc(norm_made, 1)

            def norm_for_mlp():
                mean_squares()
                step(dve.reciprocal(inv_ms, mean_eps))

            dve.wait_ge(wf_hi_made, 1)
            dve.tensor_tensor(wf_lo[:, :], wf_raw, wf_hi[:, :].bitcast(F32), ALU.subtract).then_inc(wf_made, 1)
            dve.wait_ge(gain0_in, 16)
            for tok in range(TOKS):
                dve.wait_ge(x_in[tok], 16)
                gained(tok, 0)
            for n in range(QUADS):
                for tok in range(TOKS):
                    batch_lo(tok, xT_hi, xT_lo, n)
                    if n < QUADS - 1:
                        gained(tok, n + 1)
                if n:
                    split(2 * n - 2, 2 * n, block0=True)
            split(SLOTS - 2, SLOTS, block0=True)
            norm_for_mixer()

            dve.wait_ge(gate_done, 1)
            dve.wait_ge(norm_made, 1)
            dve.wait_ge(bias_in, 16)
            for t in range(TOKS):
                f_cols = slice(t * FOX_HEADS, (t + 1) * FOX_HEADS)
                step(dve.scalar_tensor_tensor(gate_z[:, f_cols], sc[0][:, f_cols], rstd[:, t:t + 1], bias_f,
                                              ALU.mult, ALU.add))
            dve.scalar_tensor_tensor(gate_a, gate_z, -1.0, gate_z, ALU.mult, ALU.max).then_inc(gate_zed, 1)
            step(dve.tensor_scalar(gate_m, gate_z, 0.0, None, ALU.min))
            dve.wait_ge(gate_ln, 1)
            step(dve.tensor_tensor(log_f[:, :], gate_m, gate_l, ALU.subtract))

            def masked(j):
                head = T("group") * HPG
                b, p, s_bank = 2 * (j % 2), probs[j % 2], sc[j % 2]
                dve.wait_ge(score_done, head + (j + 1))
                if j >= 2:
                    dve.wait_ge(pT_done, head + (j - 1))
                dve.scalar_tensor_tensor(p[:, 0:P], s_bank[:, 0:P], c_group[:, j:j + 1], mask[:, 0:P],
                                         ALU.add, ALU.add)
                step(dve.scalar_tensor_tensor(p[:, P:3 * P], s_bank[:, P:3 * P], c_group[:, HPG + j:HPG + j + 1],
                                              mask[:, P:3 * P], ALU.add, ALU.add))
                dve.tensor_reduce(row_max[:, b:b + 1], p[:, 0:P], AX_X, ALU.max, negate=True)
                dve.tensor_reduce(row_max[:, b + 1:b + 2], p[:, P:3 * P], AX_X, ALU.max,
                                  negate=True).then_inc(score_out, 1)

            def normalised(j):
                b, p = 2 * (j % 2), probs[j % 2]
                dve.wait_ge(exp_made, T("group") * HPG + (j + 1))
                step(dve.reciprocal(row_inv[:, b:b + 2], row_sum[:, b:b + 2]))
                dve.tensor_scalar(p[:, 0:P], p[:, 0:P], row_inv[:, b:b + 1], None, ALU.mult)
                dve.tensor_scalar(p[:, P:3 * P], p[:, P:3 * P], row_inv[:, b + 1:b + 2], None,
                                  ALU.mult).then_inc(probs_made, 1)

            def group(g):
                dve.tensor_copy(log_f_group.rearrange("p (t h) -> p t h", t=TOKS),
                                log_f[:, :].rearrange("p (t h) -> p t h", t=TOKS)[:, :, bass.ds(g * HPG, HPG)]
                                ).then_inc(cum_src, 1)
                split(0, 8)
                T.up("block")
                split(0, 4)
                dve.wait_ge(cum_done, T("group", 1))
                dve.tensor_copy(c_group, sc[0][:, 0:TOKS * HPG])
                dve.tensor_scalar(negc[:, :], sc[0][0:HPG, P:3 * P], -1.0, None, ALU.mult).then_inc(cum_out, 1)
                dve.wait_ge(cum_out, T("group", 1))
                split(4, 8)
                T.up("block")
                masked(0)
                masked(1)
                normalised(0)
                masked(2)
                normalised(1)
                masked(3)
                normalised(2)
                normalised(3)
                split(0, 6)
                batch_lo(0, aT_hi, aT_lo, g)
                split(6, 8)
                T.up("block")
                T.up("group")
                batch_lo(1, aT_hi, aT_lo, g)

            T.loop(dve, GROUPS, group, block=3, hi0=1, hi1=1, step=2 * HPG, group=1)

            def add(tok, n, scale):
                dve.wait_ge(acc_done[tok], T("block", 1))
                h_cols = h[:, bass.ds(n * NB + tok * D, NB)]
                if scale is None:
                    ins = dve.tensor_tensor(h_cols, acc[tok][:, :], h_cols, ALU.add)
                else:
                    ins = dve.scalar_tensor_tensor(h_cols, acc[tok][:, :], scale[:, tok:tok + 1], h_cols,
                                                   ALU.mult, ALU.add)
                ins.then_inc(acc_out[tok], 1)

            def add_block(n, scale, batches=False, feeds=True):
                add(0, n, scale)
                if batches:
                    dve.wait_ge(acc_out[0], T("block", 1))
                    gained(0, n)
                if feeds:
                    split(0, 2)
                if batches:
                    batch_lo(0, xT_hi, xT_lo, n)
                if feeds:
                    split(2, 7)
                add(1, n, scale)
                if batches:
                    dve.wait_ge(acc_out[1], T("block", 1))
                    gained(1, n)
                if feeds:
                    split(7, 8)
                T.up("block")
                if batches:
                    batch_lo(1, xT_hi, xT_lo, n)

            def adds(scale, batches):
                if batches:
                    dve.wait_ge(gain_in, T("norm") * 16)
                    T.loop(dve, QUADS, lambda n: add_block(n, scale, True), block=1, hi0=1, hi1=1)
                else:
                    T.loop(dve, QUADS, lambda n: add_block(n, scale), block=1)

            def up_block(u):
                def squares(tok):
                    dve.wait_ge(acc_out[tok], T("block", 1))
                    dve.tensor_tensor(stage[tok][:, :], evac[tok][:, :], evac[tok][:, :],
                                      ALU.mult).then_inc(staged[tok], 1)
                squares(0)
                split(0, 2)
                batch_lo(0, aT_hi, aT_lo, u)
                split(2, 7)
                squares(1)
                split(7, 8)
                T.up("block")
                batch_lo(1, aT_hi, aT_lo, u)

            def mlp(last):
                norm_for_mlp()

                def ups():
                    T.loop(dve, QUADS, up_block, block=1, hi0=1, hi1=1)

                def chunk(i):
                    ups()
                    adds(inv_ms, False)

                T.loop(dve, SUPER - 1, chunk, block=2 * QUADS, hi0=QUADS, hi1=QUADS)
                ups()
                if last:
                    T.loop(dve, QUADS - 1, lambda n: add_block(n, inv_ms), block=1)
                    add_block(QUADS - 1, inv_ms, feeds=False)
                else:
                    adds(inv_ms, True)

            adds(None, True)
            mlp(last=False)
            norm_for_mixer()

            def rotated(tok):
                dve.wait_ge(acc_out[tok], T("block", 1))
                e = evac[tok][:, :].rearrange("p (m f d) -> p m f d", m=2, f=2)
                o = stage[tok][:, :].rearrange("p (m f d) -> p m f d", m=2, f=2)
                r = [rot[:, k * S:(k + 1) * S].rearrange("p (m d) -> p m d", m=2) for k in range(4)]
                cos, sin = (const[:, c + tok * P:c + (tok + 1) * P].unsqueeze(1).broadcast_to([P, 2, P])
                            for c in (C_COS, C_SIN))
                dve.tensor_tensor(r[0], e[:, :, 0, :], cos, ALU.mult)
                dve.tensor_tensor(r[1], e[:, :, 1, :], sin, ALU.mult)
                dve.tensor_tensor(r[2], e[:, :, 0, :], sin, ALU.mult)
                step(dve.tensor_tensor(r[3], e[:, :, 1, :], cos, ALU.mult))
                dve.tensor_tensor(o[:, :, 0, :], r[0], r[1], ALU.subtract)
                dve.tensor_tensor(o[:, :, 1, :], r[2], r[3], ALU.add).then_inc(staged[tok], 1)

            def gated_out(tok):
                dve.wait_ge(gated[tok], T("ret_head", 1))
                dve.scalar_tensor_tensor(stage[tok][:, :], mix[tok][:, :], grstd[:, tok:tok + 1], gate_r[tok],
                                         ALU.mult, ALU.mult).then_inc(staged[tok], 1)

            def ret_head(i):
                rotated(0)
                split(0, 7)
                rotated(1)
                split(7, 8)
                T.up("block")
                split(0, 4)
                dve.wait_ge(score_done, T("ret_head") + (FOX_HEADS + 1))
                dve.wait_ge(table_in, T("ret_head") * 32 + 32)
                dve.tensor_tensor(inner, sc[0][:, 0:3 * P], decay_t, ALU.mult).then_inc(inner_made, 1)
                split(4, 8)
                T.up("block")
                dve.wait_ge(gsq, T("ret_head") * TOKS + TOKS)
                dve.tensor_scalar(gmean, gsum, 1.0 / RET_V, EPS, ALU.mult, ALU.add).then_inc(gmean_made, 1)
                dve.wait_ge(groot_made, T("ret_head", 1))
                step(dve.reciprocal(grstd, groot))
                gated_out(0)
                split(0, 2)
                batch_lo(0, aT_hi, aT_lo, i)
                split(2, 7)
                gated_out(1)
                split(7, 8)
                T.up("block")
                batch_lo(1, aT_hi, aT_lo, i)
                T.up("ret_head")

            for half in range(2):
                T.loop(dve, RET_HALF, ret_head, block=3, hi0=1, hi1=1, step=3, ret_head=1)
                adds(None, half == 1)
            mlp(last=True)

            norm_for_mixer()
            dve.wait_ge(gain_in, 16 * 4)
            for t in range(TOKS):
                h_cols = h[:, t * D:(t + 1) * D]
                dve.scalar_tensor_tensor(h_cols, h_cols, rstd[:, t:t + 1], gain[:, :],
                                         ALU.mult, ALU.mult).then_inc(out_ready, 1)


def weight_stream(fox_wk, fox_wq, fox_wv, fox_wo, ret_wq, ret_wk, ret_wv, ret_wg, ret_wo, mlp_up, mlp_down):
    import numpy as np

    stream = np.empty((BLOCKS, SLOTS, P, PER_SLOT, NB), np.float32)
    count = 0

    def put(*parts):
        nonlocal count
        at = 0
        for w in parts:
            n = w.shape[1]
            stream[count, :, :, :, at:at + n] = w.reshape(SLOTS, PER_SLOT, P, n).transpose(0, 2, 1, 3)
            at += n
        count += 1

    def mlp(up, down):
        for c in range(SUPER):
            for u in range(QUADS):
                put(up[:, c * D + u * NB:c * D + (u + 1) * NB])
            for n in range(QUADS):
                put(down[c * D:(c + 1) * D, n * NB:(n + 1) * NB])

    for g in range(GROUPS):
        for w in (fox_wk, fox_wq, fox_wv):
            put(w[:, g * NB:(g + 1) * NB])
    for n in range(QUADS):
        put(fox_wo[:, n * NB:(n + 1) * NB])
    mlp(mlp_up[0], mlp_down[0])
    for half in range(2):
        for hd in range(half * RET_HALF, (half + 1) * RET_HALF):
            qk = slice(hd * RET_QK, (hd + 1) * RET_QK)
            v = slice(hd * RET_V, (hd + 1) * RET_V)
            put(ret_wq[:, qk], ret_wk[:, qk])
            put(ret_wv[:, v])
            put(ret_wg[:, v])
        for n in range(QUADS):
            put(ret_wo[half * D:(half + 1) * D, n * NB:(n + 1) * NB])
    mlp(mlp_up[1], mlp_down[1])
    assert count == BLOCKS
    return stream.reshape(BLOCKS, SLOTS, P, SW)


def shape_constants():
    import numpy as np

    table = np.zeros((P, C_END), np.float32)
    i = np.arange(P)
    table[:, C_ID:C_ID + P] = np.eye(P)
    table[:, C_TRI:C_TRI + P] = i[:, None] <= i[None, :]
    table[:, C_ONE:C_ONE + P] = 1.0
    diagonal = np.where(i[None, :] <= i[:, None], 0.0, MASKED)
    table[:, C_MASK:C_MASK + P] = diagonal
    table[:, C_MASK + 2 * P:C_MASK + 3 * P] = diagonal
    half = RET_QK // 2
    inv = np.float32(10000.0) ** (-np.arange(half, dtype=np.float32) / np.float32(half))
    for t in range(TOKS):
        angle = (np.float32(t * P) + i.astype(np.float32))[:, None] * inv[None, :]
        table[:, C_COS + t * P:C_COS + (t + 1) * P] = np.cos(angle)
        table[:, C_SIN + t * P:C_SIN + (t + 1) * P] = np.sin(angle)
    log_gamma = np.log1p(-np.exp2(-5.0 - np.arange(RET_HEADS, dtype=np.float64)))
    diff = (i[None, :] - i[:, None]).astype(np.float64)
    decay = np.zeros((RET_HEADS, P, 3 * P), np.float32)
    for hd in range(RET_HEADS):
        same = np.where(diff >= 0, np.exp(log_gamma[hd] * np.maximum(diff, 0.0)), 0.0) * RET_QK ** -0.5
        decay[hd, :, 0:P] = same
        decay[hd, :, P:2 * P] = np.exp(log_gamma[hd] * (diff + P)) * RET_QK ** -0.5
        decay[hd, :, 2 * P:] = same
    return table, decay


def kernel(x, fox_norm, fox_wq, fox_wk, fox_wv, fox_wf, fox_bf, fox_wo, ret_norm, ret_wq, ret_wk, ret_wv,
           ret_wg, ret_gn, ret_wo, mlp_norm, mlp_up, mlp_down, final_norm):
    import numpy as np
    import concourse.bacc as bacc
    from concourse.bass_utils import run_bass_kernel_spmd

    a = np.asarray
    rows = lambda v: np.broadcast_to(a(v)[..., None, :], a(v).shape[:-1] + (P, a(v).shape[-1]))
    table, decay = shape_constants()
    arrays = {
        "x": np.ascontiguousarray(a(x)[0]),
        "w_stream": weight_stream(
            a(fox_wk)[0], a(fox_wq)[0], a(fox_wv)[0], a(fox_wo)[0], a(ret_wq)[0], a(ret_wk)[0], a(ret_wv)[0],
            a(ret_wg)[0], a(ret_wo)[0], a(mlp_up), a(mlp_down)),
        "gains": np.ascontiguousarray(np.stack([
            rows(fox_norm)[0], rows(mlp_norm)[0], rows(ret_norm)[0], rows(mlp_norm)[1], rows(final_norm)])),
        "gn": np.ascontiguousarray(rows(a(ret_gn)[0].reshape(RET_HEADS, RET_V))),
        "wf": np.ascontiguousarray(a(fox_wf)[0].reshape(KT, P, FOX_HEADS).transpose(1, 0, 2).reshape(P, -1)),
        "bf": np.ascontiguousarray(rows(fox_bf)[0]),
        "consts": table,
        "decay": decay,
    }
    nc = bacc.Bacc("TRN2", target_bir_lowering=False, num_devices=1)
    ins = [nc.dram_tensor(f"in_{n}", v.shape, F32, kind="ExternalInput").ap() for n, v in arrays.items()]
    out = nc.dram_tensor("out", (S, D), F32, kind="ExternalOutput").ap()
    build_trunk(nc, *ins, out)
    r = run_bass_kernel_spmd(nc, [{f"in_{n}": v for n, v in arrays.items()}], core_ids=[0])
    return r.results[0]["out"].reshape(1, S, D)
```

```python
from contextlib import ExitStack

import concourse.bass as bass
from concourse import mybir
from concourse.alu_op_type import AluOpType as ALU

F32 = mybir.dt.float32
F32R = mybir.dt.float32r
ACT = mybir.ActivationFunctionType
AX_X = mybir.AxisListType.X

P = 128
D = 2048
S = 256
TOKS = S // P
NB = 512
KT = D // P
PER_SLOT = 2
SLOTS = KT // PER_SLOT
SW = PER_SLOT * NB
RAW = 4
QUADS = D // NB
FOX_HEADS, FOX_DIM = 16, 128
HPG = NB // FOX_DIM
GROUPS = FOX_HEADS // HPG
RET_HEADS, RET_QK, RET_V = 8, 256, 512
RET_HALF = RET_HEADS // 2
D_FF = 8192
SUPER = D_FF // D
EPS = 1e-6
MASKED = -3e38
FOX_BLOCKS = GROUPS * 3 + QUADS
MLP_BLOCKS = SUPER * 2 * QUADS
RET_BLOCKS = 2 * (RET_HALF * 3 + QUADS)
WF_COLS = KT * 2 * FOX_HEADS
BLOCKS = FOX_BLOCKS + RET_BLOCKS + 2 * MLP_BLOCKS

C_ID, C_TRI, C_ONE, C_MASK = 0, P, 2 * P, 3 * P
C_COS = C_MASK + 3 * P
C_SIN = C_COS + TOKS * P
C_END = C_SIN + TOKS * P


class Tally:

    def __init__(self, *names):
        self.base = dict.fromkeys(names, 0)
        self.off = dict.fromkeys(names, 0)

    def __call__(self, name, more=0):
        base, off = self.base[name], self.off[name] + more
        return off if isinstance(base, int) and base == 0 else base + off

    def up(self, name, by=1):
        self.off[name] += by

    def loop(self, eng, n, body, **per_round):
        before, start = dict(self.base), dict(self.off)
        with eng.Fori(0, n) as i:
            for k, d in per_round.items():
                self.base[k] = i * d + before[k]
            body(i)
        moved = {k: self.off[k] - start[k] for k in self.off if self.off[k] != start[k]}
        assert moved == per_round, (moved, per_round)
        for k, d in per_round.items():
            self.base[k] = before[k]
            self.off[k] = start[k] + n * d


def build_trunk(nc, x, w_stream, gains, gn, wf, bf, consts, decay, out):
    with ExitStack() as ctx:
        def sb(name, cols, dt=F32, parts=P):
            return ctx.enter_context(nc.sbuf_tensor(name, [parts, cols], dt))

        def sem(name):
            return ctx.enter_context(nc.semaphore(name))

        def pair(name):
            return [sem(f"{name}{t}") for t in range(TOKS)]

        h = sb("h", TOKS * D)
        xT_hi, xT_lo = sb("xT_hi", TOKS * D, F32R), sb("xT_lo", TOKS * D, F32R)
        aT_hi, aT_lo = sb("aT_hi", TOKS * D, F32R), sb("aT_lo", TOKS * D, F32R)
        raw = sb("raw", RAW * SW)
        w_hi, w_lo = sb("w_hi", SLOTS * SW, F32R), sb("w_lo", SLOTS * SW, F32R)
        const = sb("const", C_END)
        gain = sb("gain", D)
        stage = [sb(f"stage{t}", NB) for t in range(TOKS)]
        evac = [sb(f"evac{t}", NB) for t in range(TOKS)]
        wf_split = sb("wf_split", WF_COLS + P - 2 * FOX_HEADS, F32R)
        stat = sb("stat", 160)
        scratch = sb("scratch", 21 * 256)
        negc = sb("negc", S, F32, HPG)

        ident = const[:, C_ID:C_ID + P]
        tri = const[:, C_TRI:C_TRI + P]
        ones = const[:, C_ONE:C_ONE + P]
        mask = const[:, C_MASK:C_MASK + 3 * P]

        at = [0]

        def cols(n):
            at[0] += n
            return stat[:, at[0] - n:at[0]]

        sumsq = cols(TOKS * QUADS)
        mean_sq = cols(TOKS)
        mean_eps = cols(TOKS)
        inv_ms = cols(TOKS)
        root = cols(TOKS)
        rstd = cols(TOKS)
        rstd_q = cols(TOKS)
        mean_tok, mean_eps_tok, root_tok, rstd_tok = cols(TOKS), cols(TOKS), cols(TOKS), cols(TOKS)
        row_max = cols(2 * TOKS)
        row_sum = cols(2 * TOKS)
        row_inv = cols(2 * TOKS)
        gsum, gmean, groot, grstd = cols(TOKS), cols(TOKS), cols(TOKS), cols(TOKS)
        log_f_group = cols(TOKS * HPG)
        c_group = cols(TOKS * HPG)
        assert at[0] <= 160

        def cut(start, n):
            return scratch[:, start:start + n]

        kT, qT = cut(0, HPG * S), cut(1024, HPG * S)
        v_fox = [cut(2048 + t * NB, NB) for t in range(TOKS)]
        probs = [cut(3072 + b * 384, 384) for b in range(2)]
        pT = cut(3840, HPG * 384)
        wf_raw = cut(0, KT * FOX_HEADS)
        gate_z, gate_a, gate_e, gate_l, gate_m = (cut(3840 + 32 * n, 32) for n in range(5))
        gate_parts = cut(4096, TOKS * 2 * FOX_HEADS)
        gate_rows = scratch[0:2 * FOX_HEADS, 4352:4352 + S]
        log_f = sb("log_f", TOKS * FOX_HEADS)
        bias_f = cut(3840 + 32 * 6, FOX_HEADS)
        qkT = cut(0, 4 * S)
        v_ret = [cut(1024 + t * NB, NB) for t in range(TOKS)]
        gate_r = [cut(2048 + t * NB, NB) for t in range(TOKS)]
        inner = cut(3072, 384)
        decay_t = cut(3456, 384)
        gn_t = cut(3840, RET_V)
        rot = cut(4352, 4 * S)

        y = raw

        def bank(name):
            return ctx.enter_context(nc.psum_tensor(name, [P, NB], F32))

        acc = [bank(f"acc{t}") for t in range(TOKS)]
        tr = [bank(f"tr{t}") for t in range(TOKS)]
        sc = [bank(f"sc{b}") for b in range(2)]
        mix = [bank(f"mix{b}") for b in range(2)]

        raw_in = [sem(f"raw_in{r}") for r in range(RAW)]
        hi_made = sem("hi_made")
        lo_made = sem("lo_made")
        w_used = sem("w_used")
        acc_done = pair("acc_done")
        acc_out = pair("acc_out")
        staged = pair("staged")
        tr_done = pair("tr_done")
        tr_hi = pair("tr_hi")
        tr_out = pair("tr_out")
        xg_in = [sem(f"xg_in{n}") for n in range(QUADS)]
        x1_in = sem("x1_in")
        gain_in = sem("gain_in")
        ident_in, const_in = sem("ident_in"), sem("const_in")
        wf_in, bias_in = sem("wf_in"), sem("bias_in")
        wf_pad, wf_hi_made, wf_made = sem("wf_pad"), sem("wf_hi_made"), sem("wf_made")
        squared = sem("squared")
        mean_made = sem("mean_made")
        root_made = sem("root_made")
        norm_made = sem("norm_made")
        dve_step = sem("dve_step")
        gate_done, gate_out, gate_turned, gate_zed, gate_exp, gate_ln = (sem(n) for n in (
            "gate_done", "gate_out", "gate_turned", "gate_zed", "gate_exp", "gate_ln"))
        cum_src, cum_done, cum_out = sem("cum_src"), sem("cum_done"), sem("cum_out")
        score_done = sem("score_done")
        score_out = sem("score_out")
        exp_made = sem("exp_made")
        probs_made = sem("probs_made")
        pT_done, pT_out = sem("pT_done"), sem("pT_out")
        table_in = sem("table_in")
        inner_made = sem("inner_made")
        mixed = sem("mixed")
        gsq, gmean_made, groot_made, grstd_made = (sem(n) for n in (
            "gsq", "gmean_made", "groot_made", "grstd_made"))
        gated = pair("gated")
        scaled_dve, scaled_act = sem("scaled_dve"), sem("scaled_act")
        stored = sem("stored")

        block = ctx.enter_context(nc.Block())

        def wait(eng, s, value):
            if not (isinstance(value, int) and value <= 0):
                eng.wait_ge(s, value)

        def slot_cols(s, kk):
            return slice(s * SW + kk * NB, s * SW + (kk + 1) * NB)

        @block.sync
        def _(sp):
            def load_slot(s):
                if s >= RAW:
                    sp.wait_ge(lo_made, s - RAW + 1)
                sp.dma_start(raw[:, s % RAW * SW:(s % RAW + 1) * SW], w_stream[0, s]).then_inc(raw_in[s % RAW], 16)

            sp.dma_start(const[:, 0:P], consts[:, 0:P]).then_inc(ident_in, 16)
            for n in range(QUADS):
                c = slice(n * NB, (n + 1) * NB)
                sp.dma_start(h[:, c], x[0:P, c]).then_inc(xg_in[n], 16)
                sp.dma_start(gain[:, c], gains[0][:, c]).then_inc(xg_in[n], 16)
            load_slot(0)
            load_slot(1)
            sp.dma_start(h[:, D:2 * D], x[P:2 * P, :]).then_inc(x1_in, 16)
            load_slot(2)
            load_slot(3)
            load_slot(4)
            load_slot(5)
            sp.dma_start(wf_raw, wf).then_inc(wf_in, 16)
            load_slot(6)
            load_slot(7)
            sp.dma_start(const[:, P:C_END], consts[:, P:C_END]).then_inc(const_in, 16)
            with sp.Fori(1, BLOCKS) as b:
                for s in range(SLOTS):
                    sp.wait_ge(lo_made, b * SLOTS + (s - RAW + 1))
                    sp.dma_start(raw[:, s % RAW * SW:(s % RAW + 1) * SW],
                                 w_stream[bass.ds(b, 1), s].rearrange("o p n -> (o p) n")
                                 ).then_inc(raw_in[s % RAW], 16)
            sp.wait_ge(scaled_dve, 1)
            sp.dma_start(out[0:P, :], y[:, 0:D]).then_inc(stored, 16)
            for n in range(QUADS):
                if n < QUADS // 2:
                    sp.wait_ge(scaled_dve, 2 + n)
                else:
                    sp.wait_ge(scaled_act, n - QUADS // 2 + 1)
                c = slice(n * NB, (n + 1) * NB)
                sp.dma_start(out[P:2 * P, c], y[:, D + n * NB:D + (n + 1) * NB]).then_inc(stored, 16)
            sp.wait_ge(stored, 16 * (1 + QUADS))

        @block.gpsimd
        def _(pool):
            pool.memset(wf_split[:, WF_COLS:].bitcast(F32), 0.0).then_inc(wf_pad, 1)
            pool.dma_start(bias_f, bf).then_inc(bias_in, 16)
            fox_staged = QUADS + QUADS
            mlp_staged = SUPER * QUADS + QUADS
            ret_staged = RET_HEADS * 2 + QUADS
            last_use = [QUADS, fox_staged, fox_staged + mlp_staged, fox_staged + mlp_staged + ret_staged]

            def load_gain(n):
                for t in range(TOKS):
                    pool.wait_ge(staged[t], last_use[n - 1])
                pool.dma_start(gain[:, :], gains[n]).then_inc(gain_in, 16)

            load_gain(1)
            load_gain(2)
            load_gain(3)
            T = Tally("head", "block")
            T.up("block", FOX_BLOCKS + MLP_BLOCKS)

            def head(i):
                wait(pool, inner_made, T("head"))
                wait(pool, gated[1], T("head"))
                pool.dma_start(decay_t, decay[bass.ds(T("head"), 1)].rearrange("o p n -> (o p) n")
                               ).then_inc(table_in, 16)
                pool.dma_start(gn_t, gn[bass.ds(T("head"), 1)].rearrange("o p n -> (o p) n")
                               ).then_inc(table_in, 16)
                pool.wait_ge(table_in, T("head") * 32 + 32)
                for t in range(TOKS):
                    pool.wait_ge(acc_out[t], T("block") + 3)
                    pool.tensor_tensor(gate_r[t], gate_r[t], gn_t, ALU.mult).then_inc(gated[t], 1)
                T.up("head")
                T.up("block", 3)

            head(0)
            T.loop(pool, RET_HALF - 1, head, head=1, block=3)
            T.up("block", QUADS)
            T.loop(pool, RET_HALF, head, head=1, block=3)
            load_gain(4)

        @block.tensor
        def _(pe):
            T = Tally("block", "tr0", "tr1", "staged0", "staged1", "group", "ret_head")

            def product(lhs, tok, first, last, fresh=False):
                hi_t, lo_t = lhs
                for s in range(first, last):
                    if s == 0:
                        wait(pe, acc_out[tok], T("block"))
                        if fresh:
                            for t in (range(TOKS) if fresh == "both banks" else [tok]):
                                pe.wait_ge(tr_out[t], T(f"tr{t}"))
                    if tok == 0:
                        pe.wait_ge(lo_made, T("block") * SLOTS + (s + 1))
                    for kk in range(PER_SLOT):
                        kt = s * PER_SLOT + kk
                        x_cols = slice(tok * D + kt * P, tok * D + (kt + 1) * P)
                        w_cols = slot_cols(s, kk)
                        pe.matmul(acc[tok][:, :], hi_t[:, x_cols], w_hi[:, w_cols], start=(kt == 0), stop=False)
                        pe.matmul(acc[tok][:, :], hi_t[:, x_cols], w_lo[:, w_cols], start=False, stop=False)
                        m = pe.matmul(acc[tok][:, :], lo_t[:, x_cols], w_hi[:, w_cols], start=False,
                                      stop=(kt == KT - 1))
                    if s == SLOTS - 1:
                        m.then_inc(acc_done[tok], 1)
                    elif tok == TOKS - 1:
                        m.then_inc(w_used, 1)

            def batch(tok, by_act=False, blocks_ago=0):
                if by_act:
                    pe.wait_ge(acc_out[tok], T("block", 1 - blocks_ago))
                else:
                    T.up(f"staged{tok}")
                    pe.wait_ge(staged[tok], T(f"staged{tok}"))
                wait(pe, tr_out[tok], T(f"tr{tok}"))
                for j in range(NB // P):
                    m = pe.transpose(tr[tok][:, j * P:(j + 1) * P], stage[tok][:, j * P:(j + 1) * P], ident)
                m.then_inc(tr_done[tok], 1)
                T.up(f"tr{tok}")

            def run_block(lhs, mid0=None, mid1=None, fresh=False):
                product(lhs, 0, 0, 5, fresh)
                if mid0:
                    mid0()
                product(lhs, 0, 5, 8)
                product(lhs, 1, 0, 4, fresh)
                if mid1:
                    mid1()
                product(lhs, 1, 4, 8)
                T.up("block")

            xT, aT = (xT_hi, xT_lo), (aT_hi, aT_lo)
            pending = lambda: batch(1)
            own = lambda: batch(0)

            pe.wait_ge(ident_in, 16)
            for n in range(QUADS):
                batch(n % 2)

            def forget_gate():
                pe.wait_ge(wf_made, 1)
                pe.wait_ge(wf_pad, 1)
                z = sc[1][:, 0:S]
                for kt in range(KT):
                    f_cols = slice(kt * 2 * FOX_HEADS, kt * 2 * FOX_HEADS + P)
                    for x_t in (xT_hi, xT_lo):
                        x_both = x_t[:, :].rearrange("p (t d) -> p t d", t=TOKS)[:, :, kt * P:(kt + 1) * P]
                        m = pe.matmul(z, wf_split[:, f_cols], x_both, start=(kt == 0 and x_t is xT_hi),
                                      stop=(kt == KT - 1 and x_t is xT_lo))
                m.then_inc(gate_done, 1)

            def turn_gate():
                pe.wait_ge(gate_out, 1)
                rows = 2 * FOX_HEADS
                for t in range(TOKS):
                    m = pe.transpose(sc[0][:, t * rows:(t + 1) * rows], gate_rows[:, t * P:(t + 1) * P],
                                     ident[0:rows, 0:rows])
                m.then_inc(gate_turned, 1)

            def cumulate():
                pe.wait_ge(cum_src, T("group") + 1)
                f = [log_f_group[:, t * HPG:(t + 1) * HPG] for t in range(TOKS)]
                c = sc[0]
                pe.matmul(c[:, 0:HPG], tri, f[0], start=True, stop=True)
                pe.matmul(c[:, HPG:2 * HPG], ones, f[0], start=True, stop=False)
                pe.matmul(c[:, HPG:2 * HPG], tri, f[1], start=False, stop=True)
                pe.matmul(c[0:HPG, P:2 * P], f[0], tri, start=True, stop=True)
                pe.matmul(c[0:HPG, 2 * P:3 * P], f[0], ones, start=True, stop=False)
                pe.matmul(c[0:HPG, 2 * P:3 * P], f[1], tri, start=False, stop=True).then_inc(cum_done, 1)

            def scores(j):
                b = sc[j % 2]
                if j == 0:
                    pe.wait_ge(cum_out, T("group") + 1)
                    for t in range(TOKS):
                        pe.wait_ge(tr_out[t], T(f"tr{t}"))
                if j >= 2:
                    pe.wait_ge(score_out, T("group") * HPG + (j - 1))
                pick = ident[0:HPG, j:j + 1].broadcast_to([HPG, P])
                q, k = qT[:, j * S:(j + 1) * S], kT[:, j * S:(j + 1) * S]
                pe.matmul(b[:, 0:P], q[:, 0:P], k[:, 0:P], start=True, stop=False)
                pe.matmul(b[:, 0:P], pick, negc[:, 0:P], start=False, stop=True)
                pe.matmul(b[:, P:3 * P], q[:, P:S], k[:, 0:S], start=True, stop=False)
                pe.matmul(b[:, P:3 * P], pick, negc[:, 0:S], start=False, stop=True).then_inc(score_done, 1)

            def transpose_probs(j):
                b = mix[j % 2]
                pe.wait_ge(probs_made, T("group") * HPG + (j + 1))
                if j >= 2:
                    pe.wait_ge(pT_out, T("group") * HPG + (j - 1))
                for part in range(3):
                    m = pe.transpose(b[:, part * P:(part + 1) * P], probs[j % 2][:, part * P:(part + 1) * P], ident)
                m.then_inc(pT_done, 1)

            def mix_values(tok, blocks_ago):
                pe.wait_ge(acc_out[tok], T("block", 1 - blocks_ago))
                pe.wait_ge(pT_out, T("group") * HPG)
                wait(pe, tr_out[tok], T(f"tr{tok}"))
                for j in range(HPG):
                    v_cols = slice(j * FOX_DIM, (j + 1) * FOX_DIM)
                    o = tr[tok][:, j * P:(j + 1) * P]
                    pj = pT[:, j * 384:(j + 1) * 384]
                    if tok == 0:
                        m = pe.matmul(o, v_fox[0][:, v_cols], pj[:, 0:P], start=True, stop=True)
                    else:
                        pe.matmul(o, v_fox[0][:, v_cols], pj[:, P:2 * P], start=True, stop=False)
                        m = pe.matmul(o, v_fox[1][:, v_cols], pj[:, 2 * P:3 * P], start=False, stop=True)
                m.then_inc(tr_done[tok], 1)
                T.up(f"tr{tok}")

            def k_own():
                batch(0, by_act=True)

            def k_pending():
                batch(1, by_act=True, blocks_ago=1)

            def q_own_and_cum():
                k_own()
                cumulate()

            def v_block():
                product(xT, 0, 0, 2)
                k_pending()
                product(xT, 0, 2, 4)
                scores(0)
                product(xT, 0, 4, 6)
                scores(1)
                product(xT, 0, 6, 8)
                transpose_probs(0)
                scores(2)
                product(xT, 1, 0, 2)
                transpose_probs(1)
                scores(3)
                product(xT, 1, 2, 4)
                transpose_probs(2)
                product(xT, 1, 4, 6)
                transpose_probs(3)
                T.up("group")
                product(xT, 1, 6, 7)
                mix_values(0, 0)
                product(xT, 1, 7, 8)
                T.up("block")

            def mix_pending():
                mix_values(1, 1)

            product(xT, 0, 0, 3, fresh="both banks")
            batch(0)
            product(xT, 0, 3, 4)
            batch(1)
            product(xT, 0, 4, 5)
            batch(0)
            product(xT, 0, 5, 6)
            batch(1)
            product(xT, 0, 6, 8)
            product(xT, 1, 0, 4, fresh="both banks")
            k_own()
            forget_gate()
            product(xT, 1, 4, 8)
            T.up("block")
            pe.wait_ge(const_in, 16)

            def k_pending_and_gate():
                k_pending()
                turn_gate()

            def group_and_k(i):
                run_block(xT, k_pending, q_own_and_cum)
                v_block()
                run_block(xT, mix_pending, k_own)

            run_block(xT, k_pending_and_gate, q_own_and_cum)
            v_block()
            run_block(xT, mix_pending, k_own)
            T.loop(pe, GROUPS - 2, group_and_k, block=3, tr0=3, tr1=3, group=1)
            run_block(xT, k_pending, q_own_and_cum)
            v_block()
            run_block(aT, mix_pending, own, fresh=True)
            T.loop(pe, QUADS - 1, lambda i: run_block(aT, pending, own),
                   block=1, tr0=1, tr1=1, staged0=1, staged1=1)

            def mlp(last):
                run_block(xT, pending, own, fresh=True)

                def ups(i):
                    T.loop(pe, QUADS - 1, lambda i: run_block(xT, pending, own),
                           block=1, tr0=1, tr1=1, staged0=1, staged1=1)

                def chunk(i):
                    ups(i)
                    run_block(aT, pending, fresh=True)
                    T.loop(pe, QUADS - 1, lambda i: run_block(aT), block=1)
                    run_block(xT, None, own)

                T.loop(pe, SUPER - 1, chunk, block=2 * QUADS, tr0=QUADS, tr1=QUADS, staged0=QUADS, staged1=QUADS)
                ups(None)
                if last:
                    run_block(aT, pending, fresh=True)
                    T.loop(pe, QUADS - 1, lambda i: run_block(aT), block=1)
                else:
                    run_block(aT, pending, own, fresh=True)
                    T.loop(pe, QUADS - 1, lambda i: run_block(aT, pending, own),
                           block=1, tr0=1, tr1=1, staged0=1, staged1=1)

            mlp(last=False)

            def ret_scores():
                for t in range(TOKS):
                    pe.wait_ge(tr_out[t], T(f"tr{t}"))
                q = [qkT[:, dd * S:(dd + 1) * S] for dd in range(2)]
                k = [qkT[:, (2 + dd) * S:(3 + dd) * S] for dd in range(2)]
                for dd in range(2):
                    pe.matmul(sc[0][:, 0:S], k[dd][:, 0:P], q[dd], start=(dd == 0), stop=(dd == 1))
                for dd in range(2):
                    m = pe.matmul(sc[0][:, S:S + P], k[dd][:, P:S], q[dd][:, P:S], start=(dd == 0), stop=(dd == 1))
                m.then_inc(score_done, 1)
                T.up("ret_head")

            def ret_mix():
                pe.wait_ge(inner_made, T("ret_head"))
                for t in range(TOKS):
                    pe.wait_ge(acc_out[t], T("block"))
                pe.matmul(mix[0][:, :], inner[:, 0:P], v_ret[0], start=True, stop=True)
                pe.matmul(mix[1][:, :], inner[:, P:2 * P], v_ret[0], start=True, stop=False)
                pe.matmul(mix[1][:, :], inner[:, 2 * P:3 * P], v_ret[1], start=False, stop=True).then_inc(mixed, 1)

            def ret_v_and_gate(i):
                run_block(xT, pending, ret_scores)
                run_block(xT, ret_mix, own)

            def ret_head(i):
                ret_v_and_gate(i)
                run_block(xT, pending, own)

            def ret_half(first_pending, last):
                run_block(xT, first_pending, own, fresh=(first_pending is pending))
                T.loop(pe, RET_HALF - 1, ret_head, block=3, tr0=2, tr1=2, staged0=2, staged1=2, ret_head=1)
                ret_v_and_gate(None)
                if last:
                    run_block(aT, pending, own, fresh=True)
                    T.loop(pe, QUADS - 1, lambda i: run_block(aT, pending, own),
                           block=1, tr0=1, tr1=1, staged0=1, staged1=1)
                else:
                    run_block(aT, pending, fresh=True)
                    T.loop(pe, QUADS - 1, lambda i: run_block(aT), block=1)

            ret_half(pending, last=False)
            ret_half(None, last=True)
            mlp(last=True)

        @block.scalar
        def _(act):
            T = Tally("block", "tr0", "tr1", "squared", "group", "ret_head", "norm")

            def split(first, last, block0=False):
                for s in range(first, last):
                    use = s // RAW + 1
                    if block0:
                        act.wait_ge(raw_in[s % RAW], 16 * use)
                    else:
                        act.wait_ge(raw_in[s % RAW], T("block") * (16 * SLOTS // RAW) + 16 * (SLOTS // RAW + use))
                        if s == SLOTS - 1:
                            act.wait_ge(acc_done[1], T("block", 1))
                        else:
                            act.wait_ge(w_used, T("block") * (SLOTS - 1) + (s + 1))
                    act.activation(w_hi[:, s * SW:(s + 1) * SW], raw[:, s % RAW * SW:(s % RAW + 1) * SW],
                                   ACT.Copy).then_inc(hi_made, 1)

            def batch_hi(tok, dst, quad, bank=None):
                bank = tok if bank is None else bank
                T.up(f"tr{bank}")
                act.wait_ge(tr_done[bank], T(f"tr{bank}"))
                act.activation(dst[:, bass.ds(quad * NB + tok * D, NB)], tr[bank][:, :],
                               ACT.Copy).then_inc(tr_hi[bank], 1)

            def batch_qk(tok, dst):
                act.wait_ge(tr_done[tok], T(f"tr{tok}", 1))
                act.activation(dst.rearrange("p (j s) -> p j s", j=4)[:, :, tok * P:(tok + 1) * P],
                               tr[tok][:, :].rearrange("p (j s) -> p j s", j=4), ACT.Copy).then_inc(tr_out[tok], 1)
                T.up(f"tr{tok}")

            def acc_to(tok, dst, func, scale):
                act.wait_ge(acc_done[tok], T("block", 1))
                act.activation(dst, acc[tok][:, :], func, scale=scale).then_inc(acc_out[tok], 1)

            def square(tok, quad):
                wait(act, squared, T("squared"))
                act.activation(evac[tok][:, :], h[:, bass.ds(quad * NB + tok * D, NB)], ACT.Square,
                               accum_out=sumsq[:, bass.ds(quad + tok * QUADS, 1)]).then_inc(squared, 1)
                T.up("squared")

            def roots():
                T.up("norm")
                act.wait_ge(mean_made, T("norm"))
                act.activation(root, mean_eps, ACT.Sqrt).then_inc(root_made, 1)

            def factor(t, col):
                return col[:, t:t + 1]

            for n in range(QUADS):
                batch_hi(0, xT_hi, n, bank=n % 2)
                square(0, n)
            split(0, 3, block0=True)
            act.wait_ge(x1_in, 16)
            for n in range(QUADS):
                batch_hi(1, xT_hi, n, bank=n % 2)
                square(1, n)
                split(3 + n, 4 + n, block0=True)
            act.wait_ge(wf_in, 16)
            act.activation(wf_split[:, 0:WF_COLS].rearrange("p (k c h) -> p k c h", k=KT, c=2)[:, :, 0, :],
                           wf_raw.rearrange("p (k h) -> p k h", k=KT), ACT.Copy).then_inc(wf_hi_made, 1)
            split(7, 8, block0=True)
            roots()

            def proj(scale, dst):
                acc_to(0, stage[0][:, :], ACT.Copy, factor(0, scale))
                split(0, 2)
                batch_qk(0, dst)
                split(2, 7)
                acc_to(1, stage[1][:, :], ACT.Copy, factor(1, scale))
                split(7, 8)
                T.up("block")
                batch_qk(1, dst)

            def exponentials(j):
                act.wait_ge(score_out, T("group") * HPG + (j + 1))
                b, p = 2 * (j % 2), probs[j % 2]
                act.activation(p[:, 0:P], p[:, 0:P], ACT.Exp, bias=row_max[:, b:b + 1],
                               accum_out=row_sum[:, b:b + 1])
                act.activation(p[:, P:3 * P], p[:, P:3 * P], ACT.Exp, bias=row_max[:, b + 1:b + 2],
                               accum_out=row_sum[:, b + 1:b + 2]).then_inc(exp_made, 1)

            def probs_T(j):
                act.wait_ge(pT_done, T("group") * HPG + (j + 1))
                act.activation(pT[:, j * 384:(j + 1) * 384], mix[j % 2][:, 0:384], ACT.Copy).then_inc(pT_out, 1)

            def q_and_v(g):
                proj(rstd_q, qT)
                exponentials(0)
                exponentials(1)
                acc_to(0, v_fox[0], ACT.Copy, factor(0, rstd))
                exponentials(2)
                probs_T(0)
                split(0, 2)
                exponentials(3)
                probs_T(1)
                split(2, 3)
                probs_T(2)
                split(3, 4)
                probs_T(3)
                batch_hi(0, aT_hi, g)
                split(4, 7)
                acc_to(1, v_fox[1], ACT.Copy, factor(1, rstd))
                split(7, 8)
                T.up("block")
                T.up("group")
                batch_hi(1, aT_hi, g)

            def group_and_k(g):
                q_and_v(g)
                proj(rstd, kT)

            act.wait_ge(norm_made, 1)
            proj(rstd, kT)
            act.wait_ge(gate_zed, 1)
            act.activation(gate_e, gate_a, ACT.Exp, scale=-1.0).then_inc(gate_exp, 1)
            act.wait_ge(gate_exp, 1)
            act.activation(gate_l, gate_e, ACT.Ln, bias=1.0).then_inc(gate_ln, 1)
            T.loop(act, GROUPS - 1, group_and_k, block=3, tr0=3, tr1=3, group=1)
            q_and_v(GROUPS - 1)

            def add_block(n, normed=False, batches=False, feeds=True):
                if normed:
                    act.wait_ge(acc_out[0], T("block", 1))
                    square(0, n)
                if feeds:
                    split(0, 2)
                if batches:
                    batch_hi(0, xT_hi, n)
                if feeds:
                    split(2, 7)
                if normed:
                    act.wait_ge(acc_out[1], T("block", 1))
                    square(1, n)
                if feeds:
                    split(7, 8)
                T.up("block")
                if batches:
                    batch_hi(1, xT_hi, n)

            def adds(normed):
                if normed:
                    T.loop(act, QUADS, lambda n: add_block(n, normed=True, batches=True),
                           block=1, tr0=1, tr1=1, squared=2)
                else:
                    T.loop(act, QUADS, add_block, block=1)

            def up_block(u):
                acc_to(0, evac[0][:, :], ACT.Relu, 1.0)
                split(0, 2)
                batch_hi(0, aT_hi, u)
                split(2, 7)
                acc_to(1, evac[1][:, :], ACT.Relu, 1.0)
                split(7, 8)
                T.up("block")
                batch_hi(1, aT_hi, u)

            def mlp(last):
                def ups():
                    T.loop(act, QUADS, up_block, block=1, tr0=1, tr1=1)

                def chunk(i):
                    ups()
                    adds(normed=False)

                act.wait_ge(squared, T("squared"))
                T.up("norm")
                T.loop(act, SUPER - 1, chunk, block=2 * QUADS, tr0=QUADS, tr1=QUADS)
                ups()
                if last:
                    T.loop(act, QUADS - 1, lambda n: add_block(n, normed=True), block=1, squared=2)
                    for t in range(TOKS):
                        act.wait_ge(acc_out[t], T("block", 1))
                        square(t, QUADS - 1)
                        act.wait_ge(mean_made, T("norm", 1 + t))
                        act.activation(root_tok[:, t:t + 1], mean_eps_tok[:, t:t + 1], ACT.Sqrt).then_inc(root_made, 1)
                    act.wait_ge(norm_made, 4)
                    for n in range(QUADS // 2, QUADS):
                        c = y[:, D + n * NB:D + (n + 1) * NB]
                        act.activation(c, c, ACT.Copy, scale=rstd_tok[:, 1:2]).then_inc(scaled_act, 1)
                else:
                    adds(normed=True)

            adds(normed=True)
            mlp(last=False)
            roots()
            act.wait_ge(norm_made, 2)

            def ret_head(i):
                acc_to(0, evac[0][:, :], ACT.Copy, factor(0, rstd))
                split(0, 2)
                batch_qk(0, qkT)
                split(2, 7)
                acc_to(1, evac[1][:, :], ACT.Copy, factor(1, rstd))
                split(7, 8)
                T.up("block")
                batch_qk(1, qkT)
                acc_to(0, v_ret[0], ACT.Copy, factor(0, rstd))
                split(0, 7)
                acc_to(1, v_ret[1], ACT.Copy, factor(1, rstd))
                split(7, 8)
                T.up("block")
                act.wait_ge(mixed, T("ret_head", 1))
                for t in range(TOKS):
                    act.activation(gate_r[t], mix[t][:, :], ACT.Square, accum_out=gsum[:, t:t + 1]).then_inc(gsq, 1)
                act.wait_ge(gmean_made, T("ret_head", 1))
                act.activation(groot, gmean, ACT.Sqrt).then_inc(groot_made, 1)
                acc_to(0, gate_r[0], ACT.Silu, factor(0, rstd))
                split(0, 2)
                batch_hi(0, aT_hi, i)
                split(2, 7)
                acc_to(1, gate_r[1], ACT.Silu, factor(1, rstd))
                split(7, 8)
                T.up("block")
                batch_hi(1, aT_hi, i)
                T.up("ret_head")

            for half in range(2):
                T.loop(act, RET_HALF, ret_head, block=3, tr0=2, tr1=2, ret_head=1)
                adds(normed=(half == 1))
            mlp(last=True)

        @block.vector
        def _(dve):
            T = Tally("block", "hi0", "hi1", "step", "norm", "mixer_norm", "group", "ret_head")

            def step(ins):
                ins.then_inc(dve_step, 1)
                T.up("step")
                dve.wait_ge(dve_step, T("step"))

            def split(first, last, block0=False):
                for s in range(first, last):
                    dve.wait_ge(hi_made, s + 1 if block0 else T("block") * SLOTS + (SLOTS + s + 1))
                    c = slice(s * SW, (s + 1) * SW)
                    dve.tensor_tensor(w_lo[:, c], raw[:, s % RAW * SW:(s % RAW + 1) * SW],
                                      w_hi[:, c].bitcast(F32), ALU.subtract).then_inc(lo_made, 1)

            def batch_lo(tok, dst_hi, dst_lo, quad, bank=None):
                bank = tok if bank is None else bank
                T.up(f"hi{bank}")
                dve.wait_ge(tr_hi[bank], T(f"hi{bank}"))
                c = bass.ds(quad * NB + tok * D, NB)
                dve.tensor_tensor(dst_lo[:, c], tr[bank][:, :], dst_hi[:, c].bitcast(F32),
                                  ALU.subtract).then_inc(tr_out[bank], 1)

            def gained(tok, quad, bank=None):
                bank = tok if bank is None else bank
                dve.tensor_tensor(stage[bank][:, :], h[:, bass.ds(quad * NB + tok * D, NB)],
                                  gain[:, bass.ds(quad * NB, NB)], ALU.mult).then_inc(staged[bank], 1)

            def mean_squares():
                T.up("norm")
                dve.wait_ge(squared, T("norm") * TOKS * QUADS)
                step(dve.tensor_reduce(mean_sq, sumsq.rearrange("p (t n) -> p t n", t=TOKS), AX_X, ALU.add))
                dve.tensor_scalar(mean_eps, mean_sq, 1.0 / D, EPS, ALU.mult, ALU.add).then_inc(mean_made, 1)
                dve.wait_ge(mean_made, T("norm"))

            def norm_for_mixer():
                mean_squares()
                T.up("mixer_norm")
                dve.wait_ge(root_made, T("mixer_norm"))
                step(dve.reciprocal(rstd, root))
                dve.tensor_scalar(rstd_q, rstd, FOX_DIM ** -0.5, None, ALU.mult).then_inc(norm_made, 1)

            def norm_for_mlp():
                mean_squares()
                step(dve.reciprocal(inv_ms, mean_eps))

            for n in range(QUADS):
                dve.wait_ge(xg_in[n], 32)
                if n < 2:
                    gained(0, n, bank=n % 2)
                else:
                    batch_lo(0, xT_hi, xT_lo, n - 2, bank=n % 2)
                    gained(0, n, bank=n % 2)
            batch_lo(0, xT_hi, xT_lo, 2, bank=0)
            batch_lo(0, xT_hi, xT_lo, 3, bank=1)
            split(0, 2, block0=True)
            dve.wait_ge(x1_in, 16)
            gained(1, 0, bank=0)
            split(2, 3, block0=True)
            gained(1, 1, bank=1)
            for n in range(QUADS):
                batch_lo(1, xT_hi, xT_lo, n, bank=n % 2)
                if n < 2:
                    gained(1, n + 2, bank=n % 2)
                split(3 + n, 4 + n, block0=True)
            dve.wait_ge(wf_hi_made, 1)
            wf_hi, wf_lo = (wf_split[:, 0:WF_COLS].rearrange("p (k c h) -> p k c h", k=KT, c=2)[:, :, c, :]
                            for c in range(2))
            dve.tensor_tensor(wf_lo, wf_raw.rearrange("p (k h) -> p k h", k=KT), wf_hi.bitcast(F32),
                              ALU.subtract).then_inc(wf_made, 1)
            split(7, 8, block0=True)
            norm_for_mixer()

            def masked(j):
                head = T("group") * HPG
                b, p, s_bank = 2 * (j % 2), probs[j % 2], sc[j % 2]
                dve.wait_ge(score_done, head + (j + 1))
                if j >= 2:
                    dve.wait_ge(pT_done, head + (j - 1))
                dve.scalar_tensor_tensor(p[:, 0:P], s_bank[:, 0:P], c_group[:, j:j + 1], mask[:, 0:P],
                                         ALU.add, ALU.add)
                step(dve.scalar_tensor_tensor(p[:, P:3 * P], s_bank[:, P:3 * P], c_group[:, HPG + j:HPG + j + 1],
                                              mask[:, P:3 * P], ALU.add, ALU.add))
                dve.tensor_reduce(row_max[:, b:b + 1], p[:, 0:P], AX_X, ALU.max, negate=True)
                dve.tensor_reduce(row_max[:, b + 1:b + 2], p[:, P:3 * P], AX_X, ALU.max,
                                  negate=True).then_inc(score_out, 1)

            def normalised(j):
                b, p = 2 * (j % 2), probs[j % 2]
                dve.wait_ge(exp_made, T("group") * HPG + (j + 1))
                step(dve.reciprocal(row_inv[:, b:b + 2], row_sum[:, b:b + 2]))
                dve.tensor_scalar(p[:, 0:P], p[:, 0:P], row_inv[:, b:b + 1], None, ALU.mult)
                dve.tensor_scalar(p[:, P:3 * P], p[:, P:3 * P], row_inv[:, b + 1:b + 2], None,
                                  ALU.mult).then_inc(probs_made, 1)

            def k_part(middle=None):
                split(0, 5)
                if middle:
                    middle()
                split(5, 8)
                T.up("block")

            def gate_rows_out():
                dve.wait_ge(gate_done, 1)
                dve.tensor_copy(gate_rows, sc[1][0:2 * FOX_HEADS, 0:S]).then_inc(gate_out, 1)

            def log_sigmoid():
                dve.wait_ge(gate_turned, 1)
                dve.wait_ge(bias_in, 16)
                dve.wait_ge(norm_made, 1)
                step(dve.tensor_copy(gate_parts, sc[0][:, 0:TOKS * 2 * FOX_HEADS]))
                parts = gate_parts.rearrange("p (t c h) -> p t c h", t=TOKS, c=2)
                step(dve.tensor_tensor(gate_z.rearrange("p (t h) -> p t h", t=TOKS), parts[:, :, 0, :],
                                       parts[:, :, 1, :], ALU.add))
                for t in range(TOKS):
                    f_cols = slice(t * FOX_HEADS, (t + 1) * FOX_HEADS)
                    step(dve.scalar_tensor_tensor(gate_z[:, f_cols], gate_z[:, f_cols], rstd[:, t:t + 1], bias_f,
                                                  ALU.mult, ALU.add))
                dve.scalar_tensor_tensor(gate_a, gate_z, -1.0, gate_z, ALU.mult, ALU.max).then_inc(gate_zed, 1)
                step(dve.tensor_scalar(gate_m, gate_z, 0.0, None, ALU.min))
                dve.wait_ge(gate_ln, 1)
                step(dve.tensor_tensor(log_f[:, :], gate_m, gate_l, ALU.subtract))

            def q_and_v(g):
                dve.tensor_copy(log_f_group.rearrange("p (t h) -> p t h", t=TOKS),
                                log_f[:, :].rearrange("p (t h) -> p t h", t=TOKS)[:, :, bass.ds(g * HPG, HPG)]
                                ).then_inc(cum_src, 1)
                split(0, 4)
                dve.wait_ge(cum_done, T("group", 1))
                dve.tensor_copy(c_group, sc[0][:, 0:TOKS * HPG])
                dve.tensor_scalar(negc[:, :], sc[0][0:HPG, P:3 * P], -1.0, None, ALU.mult).then_inc(cum_out, 1)
                dve.wait_ge(cum_out, T("group", 1))
                split(4, 8)
                T.up("block")
                masked(0)
                masked(1)
                normalised(0)
                masked(2)
                normalised(1)
                split(0, 2)
                masked(3)
                normalised(2)
                split(2, 3)
                normalised(3)
                split(3, 4)
                batch_lo(0, aT_hi, aT_lo, g)
                split(4, 8)
                T.up("block")
                T.up("group")
                batch_lo(1, aT_hi, aT_lo, g)

            def group_and_k(g):
                q_and_v(g)
                k_part()

            k_part(gate_rows_out)
            log_sigmoid()
            dve.wait_ge(const_in, 16)
            T.loop(dve, GROUPS - 1, group_and_k, block=3, hi0=1, hi1=1, step=2 * HPG, group=1)
            q_and_v(GROUPS - 1)

            def add(tok, n, scale):
                dve.wait_ge(acc_done[tok], T("block", 1))
                h_cols = h[:, bass.ds(n * NB + tok * D, NB)]
                if scale is None:
                    ins = dve.tensor_tensor(h_cols, acc[tok][:, :], h_cols, ALU.add)
                else:
                    ins = dve.scalar_tensor_tensor(h_cols, acc[tok][:, :], scale[:, tok:tok + 1], h_cols,
                                                   ALU.mult, ALU.add)
                ins.then_inc(acc_out[tok], 1)

            def add_block(n, scale, batches=False, feeds=True):
                add(0, n, scale)
                if batches:
                    dve.wait_ge(acc_out[0], T("block", 1))
                    gained(0, n)
                if feeds:
                    split(0, 2)
                if batches:
                    batch_lo(0, xT_hi, xT_lo, n)
                if feeds:
                    split(2, 7)
                add(1, n, scale)
                if batches:
                    dve.wait_ge(acc_out[1], T("block", 1))
                    gained(1, n)
                if feeds:
                    split(7, 8)
                T.up("block")
                if batches:
                    batch_lo(1, xT_hi, xT_lo, n)

            def adds(scale, batches):
                if batches:
                    dve.wait_ge(gain_in, T("norm") * 16)
                    T.loop(dve, QUADS, lambda n: add_block(n, scale, True), block=1, hi0=1, hi1=1)
                else:
                    T.loop(dve, QUADS, lambda n: add_block(n, scale), block=1)

            def up_block(u):
                def squares(tok):
                    dve.wait_ge(acc_out[tok], T("block", 1))
                    dve.tensor_tensor(stage[tok][:, :], evac[tok][:, :], evac[tok][:, :],
                                      ALU.mult).then_inc(staged[tok], 1)
                squares(0)
                split(0, 2)
                batch_lo(0, aT_hi, aT_lo, u)
                split(2, 7)
                squares(1)
                split(7, 8)
                T.up("block")
                batch_lo(1, aT_hi, aT_lo, u)

            def mlp(last):
                norm_for_mlp()

                def ups():
                    T.loop(dve, QUADS, up_block, block=1, hi0=1, hi1=1)

                def chunk(i):
                    ups()
                    adds(inv_ms, False)

                T.loop(dve, SUPER - 1, chunk, block=2 * QUADS, hi0=QUADS, hi1=QUADS)
                ups()
                if last:
                    T.loop(dve, QUADS - 1, lambda n: add_block(n, inv_ms), block=1)
                else:
                    adds(inv_ms, True)

            adds(None, True)
            mlp(last=False)
            norm_for_mixer()

            def rotated(tok):
                dve.wait_ge(acc_out[tok], T("block", 1))
                e = evac[tok][:, :].rearrange("p (m f d) -> p m f d", m=2, f=2)
                o = stage[tok][:, :].rearrange("p (m f d) -> p m f d", m=2, f=2)
                r = [rot[:, k * S:(k + 1) * S].rearrange("p (m d) -> p m d", m=2) for k in range(4)]
                cos, sin = (const[:, c + tok * P:c + (tok + 1) * P].unsqueeze(1).broadcast_to([P, 2, P])
                            for c in (C_COS, C_SIN))
                dve.tensor_tensor(r[0], e[:, :, 0, :], cos, ALU.mult)
                dve.tensor_tensor(r[1], e[:, :, 1, :], sin, ALU.mult)
                dve.tensor_tensor(r[2], e[:, :, 0, :], sin, ALU.mult)
                step(dve.tensor_tensor(r[3], e[:, :, 1, :], cos, ALU.mult))
                dve.tensor_tensor(o[:, :, 0, :], r[0], r[1], ALU.subtract)
                dve.tensor_tensor(o[:, :, 1, :], r[2], r[3], ALU.add).then_inc(staged[tok], 1)

            def gated_out(tok):
                dve.wait_ge(gated[tok], T("ret_head", 1))
                dve.scalar_tensor_tensor(stage[tok][:, :], mix[tok][:, :], grstd[:, tok:tok + 1], gate_r[tok],
                                         ALU.mult, ALU.mult).then_inc(staged[tok], 1)

            def ret_head(i):
                rotated(0)
                split(0, 7)
                rotated(1)
                split(7, 8)
                T.up("block")
                split(0, 4)
                dve.wait_ge(score_done, T("ret_head") + (FOX_HEADS + 1))
                dve.wait_ge(table_in, T("ret_head") * 32 + 32)
                dve.tensor_tensor(inner, sc[0][:, 0:3 * P], decay_t, ALU.mult).then_inc(inner_made, 1)
                split(4, 8)
                T.up("block")
                dve.wait_ge(gsq, T("ret_head") * TOKS + TOKS)
                dve.tensor_scalar(gmean, gsum, 1.0 / RET_V, EPS, ALU.mult, ALU.add).then_inc(gmean_made, 1)
                dve.wait_ge(groot_made, T("ret_head", 1))
                step(dve.reciprocal(grstd, groot))
                gated_out(0)
                split(0, 2)
                batch_lo(0, aT_hi, aT_lo, i)
                split(2, 7)
                gated_out(1)
                split(7, 8)
                T.up("block")
                batch_lo(1, aT_hi, aT_lo, i)
                T.up("ret_head")

            for half in range(2):
                T.loop(dve, RET_HALF, ret_head, block=3, hi0=1, hi1=1, step=3, ret_head=1)
                adds(None, half == 1)
            mlp(last=True)

            def final_gain(t, n):
                c = slice(t * D + n * NB, t * D + (n + 1) * NB)
                return dve.tensor_tensor(y[:, c], h[:, c], gain[:, n * NB:(n + 1) * NB], ALU.mult)

            dve.wait_ge(gain_in, 16 * 4)
            dve.wait_ge(lo_made, BLOCKS * SLOTS)
            for t in range(TOKS):
                dve.wait_ge(acc_out[t], T("block"))
                for n in range(QUADS - 1):
                    final_gain(t, n)
            for t in range(TOKS):
                col = slice(t, t + 1)
                add(t, QUADS - 1, inv_ms)
                dve.wait_ge(acc_out[t], T("block", 1))
                step(final_gain(t, QUADS - 1))
                dve.wait_ge(squared, T("norm") * TOKS * QUADS + TOKS * (QUADS - 1) + 1 + t)
                step(dve.tensor_reduce(mean_tok[:, col], sumsq[:, t * QUADS:(t + 1) * QUADS], AX_X, ALU.add))
                dve.tensor_scalar(mean_eps_tok[:, col], mean_tok[:, col], 1.0 / D, EPS, ALU.mult,
                                  ALU.add).then_inc(mean_made, 1)
                dve.wait_ge(root_made, T("mixer_norm", 1 + t))
                dve.reciprocal(rstd_tok[:, col], root_tok[:, col]).then_inc(norm_made, 1)
                dve.wait_ge(norm_made, T("mixer_norm", 1 + t))
                pieces = [slice(0, D)] if t == 0 else [slice(D + n * NB, D + (n + 1) * NB) for n in range(QUADS // 2)]
                for c in pieces:
                    dve.tensor_scalar(y[:, c], y[:, c], rstd_tok[:, col], None, ALU.mult).then_inc(scaled_dve, 1)


def weight_stream(fox_wk, fox_wq, fox_wv, fox_wo, ret_wq, ret_wk, ret_wv, ret_wg, ret_wo, mlp_up, mlp_down):
    import numpy as np

    stream = np.empty((BLOCKS, SLOTS, P, PER_SLOT, NB), np.float32)
    count = 0

    def put(*parts):
        nonlocal count
        at = 0
        for w in parts:
            n = w.shape[1]
            stream[count, :, :, :, at:at + n] = w.reshape(SLOTS, PER_SLOT, P, n).transpose(0, 2, 1, 3)
            at += n
        count += 1

    def mlp(up, down):
        for c in range(SUPER):
            for u in range(QUADS):
                put(up[:, c * D + u * NB:c * D + (u + 1) * NB])
            for n in range(QUADS):
                put(down[c * D:(c + 1) * D, n * NB:(n + 1) * NB])

    for g in range(GROUPS):
        for w in (fox_wk, fox_wq, fox_wv):
            put(w[:, g * NB:(g + 1) * NB])
    for n in range(QUADS):
        put(fox_wo[:, n * NB:(n + 1) * NB])
    mlp(mlp_up[0], mlp_down[0])
    for half in range(2):
        for hd in range(half * RET_HALF, (half + 1) * RET_HALF):
            qk = slice(hd * RET_QK, (hd + 1) * RET_QK)
            v = slice(hd * RET_V, (hd + 1) * RET_V)
            put(ret_wq[:, qk], ret_wk[:, qk])
            put(ret_wv[:, v])
            put(ret_wg[:, v])
        for n in range(QUADS):
            put(ret_wo[half * D:(half + 1) * D, n * NB:(n + 1) * NB])
    mlp(mlp_up[1], mlp_down[1])
    assert count == BLOCKS
    return stream.reshape(BLOCKS, SLOTS, P, SW)


def shape_constants():
    import numpy as np

    table = np.zeros((P, C_END), np.float32)
    i = np.arange(P)
    table[:, C_ID:C_ID + P] = np.eye(P)
    table[:, C_TRI:C_TRI + P] = i[:, None] <= i[None, :]
    table[:, C_ONE:C_ONE + P] = 1.0
    diagonal = np.where(i[None, :] <= i[:, None], 0.0, MASKED)
    table[:, C_MASK:C_MASK + P] = diagonal
    table[:, C_MASK + 2 * P:C_MASK + 3 * P] = diagonal
    half = RET_QK // 2
    inv = np.float32(10000.0) ** (-np.arange(half, dtype=np.float32) / np.float32(half))
    for t in range(TOKS):
        angle = (np.float32(t * P) + i.astype(np.float32))[:, None] * inv[None, :]
        table[:, C_COS + t * P:C_COS + (t + 1) * P] = np.cos(angle)
        table[:, C_SIN + t * P:C_SIN + (t + 1) * P] = np.sin(angle)
    log_gamma = np.log1p(-np.exp2(-5.0 - np.arange(RET_HEADS, dtype=np.float64)))
    diff = (i[None, :] - i[:, None]).astype(np.float64)
    decay = np.zeros((RET_HEADS, P, 3 * P), np.float32)
    for hd in range(RET_HEADS):
        same = np.where(diff >= 0, np.exp(log_gamma[hd] * np.maximum(diff, 0.0)), 0.0) * RET_QK ** -0.5
        decay[hd, :, 0:P] = same
        decay[hd, :, P:2 * P] = np.exp(log_gamma[hd] * (diff + P)) * RET_QK ** -0.5
        decay[hd, :, 2 * P:] = same
    return table, decay


def kernel(x, fox_norm, fox_wq, fox_wk, fox_wv, fox_wf, fox_bf, fox_wo, ret_norm, ret_wq, ret_wk, ret_wv,
           ret_wg, ret_gn, ret_wo, mlp_norm, mlp_up, mlp_down, final_norm):
    import numpy as np
    import concourse.bacc as bacc
    from concourse.bass_utils import run_bass_kernel_spmd

    a = np.asarray
    rows = lambda v: np.broadcast_to(a(v)[..., None, :], a(v).shape[:-1] + (P, a(v).shape[-1]))
    table, decay = shape_constants()
    arrays = {
        "x": np.ascontiguousarray(a(x)[0]),
        "w_stream": weight_stream(
            a(fox_wk)[0], a(fox_wq)[0], a(fox_wv)[0], a(fox_wo)[0], a(ret_wq)[0], a(ret_wk)[0], a(ret_wv)[0],
            a(ret_wg)[0], a(ret_wo)[0], a(mlp_up), a(mlp_down)),
        "gains": np.ascontiguousarray(np.stack([
            rows(fox_norm)[0], rows(mlp_norm)[0], rows(ret_norm)[0], rows(mlp_norm)[1], rows(final_norm)])),
        "gn": np.ascontiguousarray(rows(a(ret_gn)[0].reshape(RET_HEADS, RET_V))),
        "wf": np.ascontiguousarray(a(fox_wf)[0].reshape(KT, P, FOX_HEADS).transpose(1, 0, 2).reshape(P, -1)),
        "bf": np.ascontiguousarray(rows(fox_bf)[0]),
        "consts": table,
        "decay": decay,
    }
    nc = bacc.Bacc("TRN2", target_bir_lowering=False, num_devices=1)
    ins = [nc.dram_tensor(f"in_{n}", v.shape, F32, kind="ExternalInput").ap() for n, v in arrays.items()]
    out = nc.dram_tensor("out", (S, D), F32, kind="ExternalOutput").ap()
    build_trunk(nc, *ins, out)
    r = run_bass_kernel_spmd(nc, [{f"in_{n}": v for n, v in arrays.items()}], core_ids=[0])
    return r.results[0]["out"].reshape(1, S, D)
```

```python
from contextlib import ExitStack

import concourse.bass as bass
from concourse import mybir
from concourse.alu_op_type import AluOpType as ALU

F32 = mybir.dt.float32
F32R = mybir.dt.float32r
ACT = mybir.ActivationFunctionType
AX_X = mybir.AxisListType.X

P = 128
D = 2048
S = 256
TOKS = S // P
NB = 512
KT = D // P
PER_SLOT = 2
SLOTS = KT // PER_SLOT
SW = PER_SLOT * NB
RAW = 4
QUADS = D // NB
FOX_HEADS, FOX_DIM = 16, 128
HPG = NB // FOX_DIM
GROUPS = FOX_HEADS // HPG
RET_HEADS, RET_QK, RET_V = 8, 256, 512
RET_HALF = RET_HEADS // 2
D_FF = 8192
SUPER = D_FF // D
EPS = 1e-6
MASKED = -3e38
FOX_BLOCKS = GROUPS * 3 + QUADS
MLP_BLOCKS = SUPER * 2 * QUADS
RET_BLOCKS = 2 * (RET_HALF * 3 + QUADS)
WF_COLS = KT * 2 * FOX_HEADS
BLOCKS = FOX_BLOCKS + RET_BLOCKS + 2 * MLP_BLOCKS

C_ID, C_TRI, C_ONE, C_MASK = 0, P, 2 * P, 3 * P
C_COS = C_MASK + 3 * P
C_SIN = C_COS + TOKS * P
C_PICK = C_SIN + TOKS * P
C_END = C_PICK + HPG

LO_ROW = 32
C_ROWS = LO_ROW + HPG


class Tally:

    def __init__(self, *names):
        self.base = dict.fromkeys(names, 0)
        self.off = dict.fromkeys(names, 0)

    def __call__(self, name, more=0):
        base, off = self.base[name], self.off[name] + more
        return off if isinstance(base, int) and base == 0 else base + off

    def up(self, name, by=1):
        self.off[name] += by

    def loop(self, eng, n, body, **per_round):
        before, start = dict(self.base), dict(self.off)
        with eng.Fori(0, n) as i:
            for k, d in per_round.items():
                self.base[k] = i * d + before[k]
            body(i)
        moved = {k: self.off[k] - start[k] for k in self.off if self.off[k] != start[k]}
        assert moved == per_round, (moved, per_round)
        for k, d in per_round.items():
            self.base[k] = before[k]
            self.off[k] = start[k] + n * d


def build_trunk(nc, x, w_stream, gain_t, gains, gn, wf, bf, consts, decay, out):
    with ExitStack() as ctx:
        def sb(name, cols, dt=F32, parts=P):
            return ctx.enter_context(nc.sbuf_tensor(name, [parts, cols], dt))

        def sem(name):
            return ctx.enter_context(nc.semaphore(name))

        def pair(name):
            return [sem(f"{name}{t}") for t in range(TOKS)]

        h = sb("h", TOKS * D)
        xT_hi, xT_lo = sb("xT_hi", TOKS * D, F32R), sb("xT_lo", TOKS * D, F32R)
        aT_hi, aT_lo = sb("aT_hi", TOKS * D, F32R), sb("aT_lo", TOKS * D, F32R)
        raw = sb("raw", RAW * SW)
        w_hi, w_lo = sb("w_hi", SLOTS * SW, F32R), sb("w_lo", SLOTS * SW, F32R)
        const = sb("const", C_END)
        gain = sb("gain", D)
        gain_cols = sb("gain_cols", KT)
        stage = [sb(f"stage{t}", NB) for t in range(TOKS)]
        evac = [sb(f"evac{t}", NB) for t in range(TOKS)]
        wf_split = sb("wf_split", max(WF_COLS + P - 2 * FOX_HEADS, 6 * P), F32R)
        negc = wf_split[0:C_ROWS, 0:3 * P]
        pick = wf_split[0:C_ROWS, 3 * P:3 * P + HPG]
        stat = sb("stat", 160)
        scratch = sb("scratch", 21 * 256)
        log_f_group = sb("log_f_group", TOKS * C_ROWS)

        ident = const[:, C_ID:C_ID + P]
        tri = const[:, C_TRI:C_TRI + P]
        ones = const[:, C_ONE:C_ONE + P]
        mask = const[:, C_MASK:C_MASK + 3 * P]

        at = [0]

        def cols(n):
            at[0] += n
            return stat[:, at[0] - n:at[0]]

        sumsq = cols(TOKS * QUADS)
        mean_sq = cols(TOKS)
        mean_eps = cols(TOKS)
        inv_ms = cols(TOKS)
        root = cols(TOKS)
        rstd = cols(TOKS)
        rstd_q = cols(TOKS)
        mean_tok, mean_eps_tok, root_tok, rstd_tok = cols(TOKS), cols(TOKS), cols(TOKS), cols(TOKS)
        row_max = cols(2 * TOKS)
        row_sum = cols(2 * TOKS)
        row_inv = cols(2 * TOKS)
        gsum, gmean, groot, grstd = cols(TOKS), cols(TOKS), cols(TOKS), cols(TOKS)
        c_group = cols(TOKS * HPG)
        assert at[0] <= 160

        def cut(start, n):
            return scratch[:, start:start + n]

        kT, qT = cut(0, HPG * S), cut(1024, HPG * S)
        v_fox = [cut(2048 + t * NB, NB) for t in range(TOKS)]
        probs = [cut(3072 + b * 384, 384) for b in range(2)]
        pT = cut(3840, HPG * 384)
        wf_raw = cut(0, KT * FOX_HEADS)
        gate_z, gate_a, gate_e, gate_l, gate_m = (cut(3840 + 32 * n, 32) for n in range(5))
        gate_parts = cut(4096, TOKS * 2 * FOX_HEADS)
        gate_rows = scratch[0:2 * FOX_HEADS, 4352:4352 + S]
        log_f = sb("log_f", TOKS * FOX_HEADS)
        bias_f = cut(3840 + 32 * 6, FOX_HEADS)
        qkT = cut(0, 4 * S)
        v_hi, v_lo = ([part[:, (t + 1) * D - NB:(t + 1) * D] for t in range(TOKS)] for part in (aT_hi, aT_lo))
        gate_r = [cut(2048 + t * NB, NB) for t in range(TOKS)]
        inner = cut(3072, 384)
        inner_hi, inner_lo = wf_split[:, 0:3 * P], wf_split[:, 3 * P:6 * P]
        decay_t = cut(3456, 384)
        gn_t = cut(3840, RET_V)
        rot = cut(4352, 4 * S)

        y = raw

        def bank(name):
            return ctx.enter_context(nc.psum_tensor(name, [P, NB], F32))

        acc = [bank(f"acc{t}") for t in range(TOKS)]
        tr = [bank(f"tr{t}") for t in range(TOKS)]
        sc = [bank(f"sc{b}") for b in range(2)]
        mix = [bank(f"mix{b}") for b in range(2)]

        raw_in = [sem(f"raw_in{r}") for r in range(RAW)]
        hi_made = sem("hi_made")
        lo_made = sem("lo_made")
        w_used = sem("w_used")
        acc_done = pair("acc_done")
        acc_out = pair("acc_out")
        staged = pair("staged")
        tr_done = pair("tr_done")
        tr_hi = pair("tr_hi")
        tr_out = pair("tr_out")
        gain_cols_in = sem("gain_cols_in")
        x0_in = [sem(f"x0_in{n}") for n in range(QUADS)]
        x1_in = sem("x1_in")
        gain_in = sem("gain_in")
        ident_in, const_in = sem("ident_in"), sem("const_in")
        wf_in, bias_in = sem("wf_in"), sem("bias_in")
        zeros_set = sem("zeros_set")
        wf_hi_made, wf_made = sem("wf_hi_made"), sem("wf_made")
        squared = sem("squared")
        mean_made = sem("mean_made")
        root_made = sem("root_made")
        norm_made = sem("norm_made")
        dve_step = sem("dve_step")
        gate_done, gate_out, gate_turned, gate_zed, gate_exp, gate_ln = (sem(n) for n in (
            "gate_done", "gate_out", "gate_turned", "gate_zed", "gate_exp", "gate_ln"))
        cum_src, cum_done, cum_out = sem("cum_src"), sem("cum_done"), sem("cum_out")
        score_done = sem("score_done")
        score_out = sem("score_out")
        exp_made = sem("exp_made")
        probs_made = sem("probs_made")
        pT_done, pT_out = sem("pT_done"), sem("pT_out")
        table_in = sem("table_in")
        inner_made = sem("inner_made")
        v_hi_made = pair("v_hi_made")
        mixed = sem("mixed")
        gsq, gmean_made, groot_made, grstd_made = (sem(n) for n in (
            "gsq", "gmean_made", "groot_made", "grstd_made"))
        gated = pair("gated")
        scaled_dve, scaled_act = sem("scaled_dve"), sem("scaled_act")
        stored = sem("stored")

        block = ctx.enter_context(nc.Block())

        def wait(eng, s, value):
            if not (isinstance(value, int) and value <= 0):
                eng.wait_ge(s, value)

        def slot_cols(s, kk):
            return slice(s * SW + kk * NB, s * SW + (kk + 1) * NB)

        @block.sync
        def _(sp):
            def load_slot(s):
                if s >= RAW:
                    sp.wait_ge(lo_made, s - RAW + 1)
                sp.dma_start(raw[:, s % RAW * SW:(s % RAW + 1) * SW], w_stream[0, s]).then_inc(raw_in[s % RAW], 16)

            sp.dma_start(const[:, 0:P], consts[:, 0:P]).then_inc(ident_in, 16)
            sp.dma_start(gain_cols[:, :], gain_t).then_inc(gain_cols_in, 16)
            for n in range(QUADS):
                c = slice(n * NB, (n + 1) * NB)
                sp.dma_start(h[:, c], x[0:P, c]).then_inc(x0_in[n], 16)
            load_slot(0)
            load_slot(1)
            load_slot(2)
            load_slot(3)
            sp.dma_start(h[:, D:2 * D], x[P:2 * P, :]).then_inc(x1_in, 16)
            load_slot(4)
            load_slot(5)
            sp.dma_start(wf_raw, wf).then_inc(wf_in, 16)
            load_slot(6)
            load_slot(7)
            sp.dma_start(const[:, P:C_END], consts[:, P:C_END]).then_inc(const_in, 16)
            with sp.Fori(1, BLOCKS) as b:
                for s in range(SLOTS):
                    sp.wait_ge(lo_made, b * SLOTS + (s - RAW + 1))
                    sp.dma_start(raw[:, s % RAW * SW:(s % RAW + 1) * SW],
                                 w_stream[bass.ds(b, 1), s].rearrange("o p n -> (o p) n")
                                 ).then_inc(raw_in[s % RAW], 16)
            sp.wait_ge(scaled_dve, 1)
            sp.dma_start(out[0:P, :], y[:, 0:D]).then_inc(stored, 16)
            for n in range(QUADS):
                if n < QUADS // 2:
                    sp.wait_ge(scaled_dve, 2 + n)
                else:
                    sp.wait_ge(scaled_act, n - QUADS // 2 + 1)
                c = slice(n * NB, (n + 1) * NB)
                sp.dma_start(out[P:2 * P, c], y[:, D + n * NB:D + (n + 1) * NB]).then_inc(stored, 16)
            sp.wait_ge(stored, 16 * (1 + QUADS))

        @block.gpsimd
        def _(pool):
            pool.memset(wf_split[:, WF_COLS:].bitcast(F32), 0.0).then_inc(zeros_set, 1)
            pool.memset(log_f_group[:, :], 0.0).then_inc(zeros_set, 1)
            pool.dma_start(bias_f, bf).then_inc(bias_in, 16)
            fox_staged = QUADS
            mlp_staged = SUPER * QUADS + QUADS
            ret_staged = RET_HEADS * 2 + QUADS
            last_use = [0, fox_staged, fox_staged + mlp_staged, fox_staged + mlp_staged + ret_staged]

            def load_gain(n):
                for t in range(TOKS):
                    wait(pool, staged[t], last_use[n])
                pool.dma_start(gain[:, :], gains[n]).then_inc(gain_in, 16)

            pool.wait_ge(lo_made, SLOTS)
            load_gain(0)
            load_gain(1)
            load_gain(2)
            T = Tally("head", "block")
            T.up("block", FOX_BLOCKS + MLP_BLOCKS)

            def head(i):
                wait(pool, inner_made, T("head"))
                wait(pool, gated[1], T("head"))
                pool.dma_start(decay_t, decay[bass.ds(T("head"), 1)].rearrange("o p n -> (o p) n")
                               ).then_inc(table_in, 16)
                pool.dma_start(gn_t, gn[bass.ds(T("head"), 1)].rearrange("o p n -> (o p) n")
                               ).then_inc(table_in, 16)
                pool.wait_ge(table_in, T("head") * 32 + 32)
                for t in range(TOKS):
                    pool.wait_ge(acc_out[t], T("block") + 3)
                    pool.tensor_tensor(gate_r[t], gate_r[t], gn_t, ALU.mult).then_inc(gated[t], 1)
                T.up("head")
                T.up("block", 3)

            head(0)
            T.loop(pool, RET_HALF - 1, head, head=1, block=3)
            T.up("block", QUADS)
            T.loop(pool, RET_HALF, head, head=1, block=3)
            load_gain(3)

        @block.tensor
        def _(pe):
            T = Tally("block", "tr0", "tr1", "staged0", "staged1", "group", "ret_head")

            def product(lhs, tok, first, last, fresh=False):
                hi_t, lo_t = lhs
                for s in range(first, last):
                    if s == 0:
                        wait(pe, acc_out[tok], T("block"))
                        if fresh is True:
                            pe.wait_ge(tr_out[tok], T(f"tr{tok}"))
                    if fresh == "by quads" and s * PER_SLOT % (NB // P) == 0:
                        n = s * PER_SLOT // (NB // P)
                        pe.wait_ge(tr_out[n % 2], (tok * QUADS + n) // 2 + 1)
                    if tok == 0:
                        pe.wait_ge(lo_made, T("block") * SLOTS + (s + 1))
                    for kk in range(PER_SLOT):
                        kt = s * PER_SLOT + kk
                        x_cols = slice(tok * D + kt * P, tok * D + (kt + 1) * P)
                        w_cols = slot_cols(s, kk)
                        pe.matmul(acc[tok][:, :], hi_t[:, x_cols], w_hi[:, w_cols], start=(kt == 0), stop=False)
                        pe.matmul(acc[tok][:, :], hi_t[:, x_cols], w_lo[:, w_cols], start=False, stop=False)
                        m = pe.matmul(acc[tok][:, :], lo_t[:, x_cols], w_hi[:, w_cols], start=False,
                                      stop=(kt == KT - 1))
                    if s == SLOTS - 1:
                        m.then_inc(acc_done[tok], 1)
                    elif tok == TOKS - 1:
                        m.then_inc(w_used, 1)

            def batch(tok, by_act=False, blocks_ago=0):
                if by_act:
                    pe.wait_ge(acc_out[tok], T("block", 1 - blocks_ago))
                else:
                    T.up(f"staged{tok}")
                    pe.wait_ge(staged[tok], T(f"staged{tok}"))
                wait(pe, tr_out[tok], T(f"tr{tok}"))
                for j in range(NB // P):
                    m = pe.transpose(tr[tok][:, j * P:(j + 1) * P], stage[tok][:, j * P:(j + 1) * P], ident)
                m.then_inc(tr_done[tok], 1)
                T.up(f"tr{tok}")

            def run_block(lhs, mid0=None, mid1=None, fresh=False):
                product(lhs, 0, 0, 5, fresh)
                if mid0:
                    mid0()
                product(lhs, 0, 5, 8)
                product(lhs, 1, 0, 4, fresh)
                if mid1:
                    mid1()
                product(lhs, 1, 4, 8)
                T.up("block")

            xT, aT = (xT_hi, xT_lo), (aT_hi, aT_lo)
            pending = lambda: batch(1)
            own = lambda: batch(0)

            def batch_of_x(tok, n):
                pe.wait_ge(x0_in[n] if tok == 0 else x1_in, 16)
                wait(pe, tr_out[n % 2], T(f"tr{n % 2}"))
                for j in range(NB // P):
                    c = tok * D + n * NB + j * P
                    m = pe.transpose(tr[n % 2][:, j * P:(j + 1) * P], h[:, c:c + P], ident)
                m.then_inc(tr_done[n % 2], 1)
                T.up(f"tr{n % 2}")

            pe.wait_ge(ident_in, 16)
            pe.wait_ge(gain_cols_in, 16)
            for n in range(QUADS):
                batch_of_x(0, n)

            def forget_gate():
                pe.wait_ge(wf_made, 1)
                pe.wait_ge(zeros_set, 2)
                z = sc[1][:, 0:S]
                for kt in range(KT):
                    f_cols = slice(kt * 2 * FOX_HEADS, kt * 2 * FOX_HEADS + P)
                    for x_t in (xT_hi, xT_lo):
                        x_both = x_t[:, :].rearrange("p (t d) -> p t d", t=TOKS)[:, :, kt * P:(kt + 1) * P]
                        m = pe.matmul(z, wf_split[:, f_cols], x_both, start=(kt == 0 and x_t is xT_hi),
                                      stop=(kt == KT - 1 and x_t is xT_lo))
                m.then_inc(gate_done, 1)

            def turn_gate():
                pe.wait_ge(gate_out, 1)
                rows = 2 * FOX_HEADS
                for t in range(TOKS):
                    m = pe.transpose(sc[0][:, t * rows:(t + 1) * rows], gate_rows[:, t * P:(t + 1) * P],
                                     ident[0:rows, 0:rows])
                m.then_inc(gate_turned, 1)

            def cumulate():
                pe.wait_ge(cum_src, T("group") + 1)
                rows = [log_f_group[:, t * C_ROWS:(t + 1) * C_ROWS] for t in range(TOKS)]
                f = [r[:, 0:HPG] for r in rows]
                c = sc[0]
                pe.matmul(c[:, 0:HPG], tri, f[0], start=True, stop=True)
                pe.matmul(c[:, HPG:2 * HPG], ones, f[0], start=True, stop=False)
                pe.matmul(c[:, HPG:2 * HPG], tri, f[1], start=False, stop=True)
                pe.matmul(c[0:C_ROWS, P:2 * P], rows[0], tri, start=True, stop=True)
                pe.matmul(c[0:C_ROWS, 2 * P:3 * P], rows[0], ones, start=True, stop=False)
                pe.matmul(c[0:C_ROWS, 2 * P:3 * P], rows[1], tri, start=False, stop=True).then_inc(cum_done, 1)

            def scores(j):
                b = sc[j % 2]
                if j == 0:
                    pe.wait_ge(cum_out, T("group") + 1)
                    for t in range(TOKS):
                        pe.wait_ge(tr_out[t], T(f"tr{t}"))
                if j >= 2:
                    pe.wait_ge(score_out, T("group") * HPG + (j - 1))
                ones_at_j = pick[:, j:j + 1].broadcast_to([C_ROWS, P])
                q, k = qT[:, j * S:(j + 1) * S], kT[:, j * S:(j + 1) * S]
                pe.matmul(b[:, 0:3 * P], ones_at_j, negc, start=True, stop=False)
                pe.matmul(b[:, 0:P], q[:, 0:P], k[:, 0:P], start=False, stop=False)
                pe.matmul(b[:, P:3 * P], q[:, P:S], k[:, 0:S], start=False, stop=True).then_inc(score_done, 1)

            def transpose_probs(j):
                b = mix[j % 2]
                pe.wait_ge(probs_made, T("group") * HPG + (j + 1))
                if j >= 2:
                    pe.wait_ge(pT_out, T("group") * HPG + (j - 1))
                for part in range(3):
                    m = pe.transpose(b[:, part * P:(part + 1) * P], probs[j % 2][:, part * P:(part + 1) * P], ident)
                m.then_inc(pT_done, 1)

            def mix_values(tok, blocks_ago):
                pe.wait_ge(acc_out[tok], T("block", 1 - blocks_ago))
                pe.wait_ge(pT_out, T("group") * HPG)
                wait(pe, tr_out[tok], T(f"tr{tok}"))
                for j in range(HPG):
                    v_cols = slice(j * FOX_DIM, (j + 1) * FOX_DIM)
                    o = tr[tok][:, j * P:(j + 1) * P]
                    pj = pT[:, j * 384:(j + 1) * 384]
                    if tok == 0:
                        m = pe.matmul(o, v_fox[0][:, v_cols], pj[:, 0:P], start=True, stop=True)
                    else:
                        pe.matmul(o, v_fox[0][:, v_cols], pj[:, P:2 * P], start=True, stop=False)
                        m = pe.matmul(o, v_fox[1][:, v_cols], pj[:, 2 * P:3 * P], start=False, stop=True)
                m.then_inc(tr_done[tok], 1)
                T.up(f"tr{tok}")

            def k_own():
                batch(0, by_act=True)

            def k_pending():
                batch(1, by_act=True, blocks_ago=1)

            def q_own_and_cum():
                k_own()
                cumulate()

            def v_block():
                product(xT, 0, 0, 1)
                k_pending()
                product(xT, 0, 1, 3)
                scores(0)
                product(xT, 0, 3, 5)
                scores(1)
                product(xT, 0, 5, 6)
                transpose_probs(0)
                product(xT, 0, 6, 7)
                scores(2)
                product(xT, 0, 7, 8)
                transpose_probs(1)
                scores(3)
                product(xT, 1, 0, 2)
                transpose_probs(2)
                product(xT, 1, 2, 5)
                transpose_probs(3)
                T.up("group")
                product(xT, 1, 5, 7)
                mix_values(0, 0)
                product(xT, 1, 7, 8)
                T.up("block")

            def mix_pending():
                mix_values(1, 1)

            product(xT, 0, 0, 3, fresh="by quads")
            batch_of_x(1, 0)
            batch_of_x(1, 1)
            product(xT, 0, 3, 4, fresh="by quads")
            product(xT, 1, 0, 1, fresh="by quads")
            batch_of_x(1, 2)
            product(xT, 1, 1, 2, fresh="by quads")
            batch_of_x(1, 3)
            product(xT, 1, 2, 4, fresh="by quads")
            product(xT, 0, 4, 8, fresh="by quads")
            product(xT, 1, 4, 7, fresh="by quads")
            forget_gate()
            k_own()
            product(xT, 1, 7, 8, fresh="by quads")
            T.up("block")
            pe.wait_ge(const_in, 16)

            def k_pending_and_gate():
                k_pending()
                turn_gate()

            def group_and_k(i):
                run_block(xT, k_pending, q_own_and_cum)
                v_block()
                run_block(xT, mix_pending, k_own)

            run_block(xT, k_pending_and_gate, q_own_and_cum)
            v_block()
            run_block(xT, mix_pending, k_own)
            T.loop(pe, GROUPS - 2, group_and_k, block=3, tr0=3, tr1=3, group=1)
            run_block(xT, k_pending, q_own_and_cum)
            v_block()
            run_block(aT, mix_pending, own, fresh=True)
            T.loop(pe, QUADS - 1, lambda i: run_block(aT, pending, own),
                   block=1, tr0=1, tr1=1, staged0=1, staged1=1)

            def mlp(last):
                run_block(xT, pending, own, fresh=True)

                def ups(i):
                    T.loop(pe, QUADS - 1, lambda i: run_block(xT, pending, own),
                           block=1, tr0=1, tr1=1, staged0=1, staged1=1)

                def chunk(i):
                    ups(i)
                    run_block(aT, pending, fresh=True)
                    T.loop(pe, QUADS - 1, lambda i: run_block(aT), block=1)
                    run_block(xT, None, own)

                T.loop(pe, SUPER - 1, chunk, block=2 * QUADS, tr0=QUADS, tr1=QUADS, staged0=QUADS, staged1=QUADS)
                ups(None)
                if last:
                    run_block(aT, pending, fresh=True)
                    T.loop(pe, QUADS - 1, lambda i: run_block(aT), block=1)
                else:
                    run_block(aT, pending, own, fresh=True)
                    T.loop(pe, QUADS - 1, lambda i: run_block(aT, pending, own),
                           block=1, tr0=1, tr1=1, staged0=1, staged1=1)

            mlp(last=False)

            def ret_scores():
                for t in range(TOKS):
                    pe.wait_ge(tr_out[t], T(f"tr{t}"))
                q = [qkT[:, dd * S:(dd + 1) * S] for dd in range(2)]
                k = [qkT[:, (2 + dd) * S:(3 + dd) * S] for dd in range(2)]
                for dd in range(2):
                    pe.matmul(sc[0][:, 0:S], k[dd][:, 0:P], q[dd], start=(dd == 0), stop=(dd == 1))
                for dd in range(2):
                    m = pe.matmul(sc[0][:, S:S + P], k[dd][:, P:S], q[dd][:, P:S], start=(dd == 0), stop=(dd == 1))
                m.then_inc(score_done, 1)
                T.up("ret_head")

            def ret_mix():
                pe.wait_ge(inner_made, T("ret_head"))
                for t in range(TOKS):
                    pe.wait_ge(acc_out[t], T("block"))

                def mix_one(t, part, v_t, first, last):
                    c = slice(part * P, (part + 1) * P)
                    pe.matmul(mix[t][:, :], inner_hi[:, c], v_hi[v_t], start=first, stop=False)
                    pe.matmul(mix[t][:, :], inner_hi[:, c], v_lo[v_t], start=False, stop=False)
                    return pe.matmul(mix[t][:, :], inner_lo[:, c], v_hi[v_t], start=False, stop=last)

                mix_one(0, 0, 0, True, True)
                mix_one(1, 1, 0, True, False)
                mix_one(1, 2, 1, False, True).then_inc(mixed, 1)

            def ret_v_and_gate(i):
                run_block(xT, pending, ret_scores)
                run_block(xT, ret_mix, own)

            def ret_head(i):
                ret_v_and_gate(i)
                run_block(xT, pending, own)

            def ret_half(first_pending, last):
                run_block(xT, first_pending, own, fresh=(first_pending is pending))
                T.loop(pe, RET_HALF - 1, ret_head, block=3, tr0=2, tr1=2, staged0=2, staged1=2, ret_head=1)
                ret_v_and_gate(None)
                if last:
                    run_block(aT, pending, own, fresh=True)
                    T.loop(pe, QUADS - 1, lambda i: run_block(aT, pending, own),
                           block=1, tr0=1, tr1=1, staged0=1, staged1=1)
                else:
                    run_block(aT, pending, fresh=True)
                    T.loop(pe, QUADS - 1, lambda i: run_block(aT), block=1)

            ret_half(pending, last=False)
            ret_half(None, last=True)
            mlp(last=True)

        @block.scalar
        def _(act):
            T = Tally("block", "tr0", "tr1", "squared", "group", "ret_head", "norm")

            def split(first, last, block0=False):
                for s in range(first, last):
                    use = s // RAW + 1
                    if block0:
                        act.wait_ge(raw_in[s % RAW], 16 * use)
                    else:
                        act.wait_ge(raw_in[s % RAW], T("block") * (16 * SLOTS // RAW) + 16 * (SLOTS // RAW + use))
                        if s == SLOTS - 1:
                            act.wait_ge(acc_done[1], T("block", 1))
                        else:
                            act.wait_ge(w_used, T("block") * (SLOTS - 1) + (s + 1))
                    act.activation(w_hi[:, s * SW:(s + 1) * SW], raw[:, s % RAW * SW:(s % RAW + 1) * SW],
                                   ACT.Copy).then_inc(hi_made, 1)

            def batch_hi(tok, dst, quad):
                T.up(f"tr{tok}")
                act.wait_ge(tr_done[tok], T(f"tr{tok}"))
                act.activation(dst[:, bass.ds(quad * NB + tok * D, NB)], tr[tok][:, :],
                               ACT.Copy).then_inc(tr_hi[tok], 1)

            def batch_qk(tok, dst):
                act.wait_ge(tr_done[tok], T(f"tr{tok}", 1))
                act.activation(dst.rearrange("p (j s) -> p j s", j=4)[:, :, tok * P:(tok + 1) * P],
                               tr[tok][:, :].rearrange("p (j s) -> p j s", j=4), ACT.Copy).then_inc(tr_out[tok], 1)
                T.up(f"tr{tok}")

            def acc_to(tok, dst, func, scale):
                act.wait_ge(acc_done[tok], T("block", 1))
                act.activation(dst, acc[tok][:, :], func, scale=scale).then_inc(acc_out[tok], 1)

            def square(tok, quad):
                wait(act, squared, T("squared"))
                act.activation(evac[tok][:, :], h[:, bass.ds(quad * NB + tok * D, NB)], ACT.Square,
                               accum_out=sumsq[:, bass.ds(quad + tok * QUADS, 1)]).then_inc(squared, 1)
                T.up("squared")

            def roots():
                T.up("norm")
                act.wait_ge(mean_made, T("norm"))
                act.activation(root, mean_eps, ACT.Sqrt).then_inc(root_made, 1)

            def factor(t, col):
                return col[:, t:t + 1]

            def x_hi(tok, n):
                T.up(f"tr{n % 2}")
                act.wait_ge(tr_done[n % 2], T(f"tr{n % 2}"))
                for j in range(NB // P):
                    kt = n * (NB // P) + j
                    c = slice(tok * D + kt * P, tok * D + (kt + 1) * P)
                    ins = act.activation(xT_hi[:, c], tr[n % 2][:, j * P:(j + 1) * P], ACT.Copy,
                                         scale=gain_cols[:, kt:kt + 1])
                ins.then_inc(tr_hi[n % 2], 1)

            x_hi(0, 0)
            x_hi(0, 1)
            split(0, 1, block0=True)
            x_hi(0, 2)
            split(1, 2, block0=True)
            x_hi(0, 3)
            split(2, 3, block0=True)
            square(0, 0)
            split(3, 4, block0=True)
            square(0, 1)
            act.wait_ge(x1_in, 16)
            x_hi(1, 0)
            x_hi(1, 1)
            split(4, 5, block0=True)
            x_hi(1, 2)
            x_hi(1, 3)
            split(5, 6, block0=True)
            square(0, 2)
            split(6, 7, block0=True)
            square(0, 3)
            square(1, 0)
            act.wait_ge(wf_in, 16)
            act.activation(wf_split[:, 0:WF_COLS].rearrange("p (k c h) -> p k c h", k=KT, c=2)[:, :, 0, :],
                           wf_raw.rearrange("p (k h) -> p k h", k=KT), ACT.Copy).then_inc(wf_hi_made, 1)
            split(7, 8, block0=True)
            for n in range(1, QUADS):
                square(1, n)
            roots()

            def proj(scale, dst):
                acc_to(0, stage[0][:, :], ACT.Copy, factor(0, scale))
                split(0, 2)
                batch_qk(0, dst)
                split(2, 6)
                acc_to(1, stage[1][:, :], ACT.Copy, factor(1, scale))
                split(6, 8)
                T.up("block")
                batch_qk(1, dst)

            def exponentials(j):
                act.wait_ge(score_out, T("group") * HPG + (j + 1))
                b, p = 2 * (j % 2), probs[j % 2]
                act.activation(p[:, 0:P], p[:, 0:P], ACT.Exp, bias=row_max[:, b:b + 1],
                               accum_out=row_sum[:, b:b + 1])
                act.activation(p[:, P:3 * P], p[:, P:3 * P], ACT.Exp, bias=row_max[:, b + 1:b + 2],
                               accum_out=row_sum[:, b + 1:b + 2]).then_inc(exp_made, 1)

            def probs_T(j):
                act.wait_ge(pT_done, T("group") * HPG + (j + 1))
                act.activation(pT[:, j * 384:(j + 1) * 384], mix[j % 2][:, 0:384], ACT.Copy).then_inc(pT_out, 1)

            def q_and_v(g):
                proj(rstd_q, qT)
                exponentials(0)
                exponentials(1)
                probs_T(0)
                acc_to(0, v_fox[0], ACT.Copy, factor(0, rstd))
                exponentials(2)
                probs_T(1)
                exponentials(3)
                split(0, 1)
                probs_T(2)
                split(1, 3)
                probs_T(3)
                split(3, 4)
                batch_hi(0, aT_hi, g)
                split(4, 7)
                acc_to(1, v_fox[1], ACT.Copy, factor(1, rstd))
                split(7, 8)
                T.up("block")
                T.up("group")
                batch_hi(1, aT_hi, g)

            def group_and_k(g):
                q_and_v(g)
                proj(rstd, kT)

            act.wait_ge(norm_made, 1)
            proj(rstd, kT)
            act.wait_ge(gate_zed, 1)
            act.activation(gate_e, gate_a, ACT.Exp, scale=-1.0).then_inc(gate_exp, 1)
            act.wait_ge(gate_exp, 1)
            act.activation(gate_l, gate_e, ACT.Ln, bias=1.0).then_inc(gate_ln, 1)
            T.loop(act, GROUPS - 1, group_and_k, block=3, tr0=3, tr1=3, group=1)
            q_and_v(GROUPS - 1)

            def add_block(n, normed=False, batches=False, feeds=True):
                if normed:
                    act.wait_ge(acc_out[0], T("block", 1))
                    square(0, n)
                if feeds:
                    split(0, 2)
                if batches:
                    batch_hi(0, xT_hi, n)
                if feeds:
                    split(2, 7)
                if normed:
                    act.wait_ge(acc_out[1], T("block", 1))
                    square(1, n)
                if feeds:
                    split(7, 8)
                T.up("block")
                if batches:
                    batch_hi(1, xT_hi, n)

            def adds(normed):
                if normed:
                    T.loop(act, QUADS, lambda n: add_block(n, normed=True, batches=True),
                           block=1, tr0=1, tr1=1, squared=2)
                else:
                    T.loop(act, QUADS, add_block, block=1)

            def up_block(u):
                acc_to(0, evac[0][:, :], ACT.Relu, 1.0)
                split(0, 2)
                batch_hi(0, aT_hi, u)
                split(2, 7)
                acc_to(1, evac[1][:, :], ACT.Relu, 1.0)
                split(7, 8)
                T.up("block")
                batch_hi(1, aT_hi, u)

            def mlp(last):
                def ups():
                    T.loop(act, QUADS, up_block, block=1, tr0=1, tr1=1)

                def chunk(i):
                    ups()
                    adds(normed=False)

                act.wait_ge(squared, T("squared"))
                T.up("norm")
                T.loop(act, SUPER - 1, chunk, block=2 * QUADS, tr0=QUADS, tr1=QUADS)
                ups()
                if last:
                    T.loop(act, QUADS - 1, lambda n: add_block(n, normed=True), block=1, squared=2)
                    for t in range(TOKS):
                        act.wait_ge(acc_out[t], T("block", 1))
                        square(t, QUADS - 1)
                        act.wait_ge(mean_made, T("norm", 1 + t))
                        act.activation(root_tok[:, t:t + 1], mean_eps_tok[:, t:t + 1], ACT.Sqrt).then_inc(root_made, 1)
                    act.wait_ge(norm_made, 4)
                    for n in range(QUADS // 2, QUADS):
                        c = y[:, D + n * NB:D + (n + 1) * NB]
                        act.activation(c, c, ACT.Copy, scale=rstd_tok[:, 1:2]).then_inc(scaled_act, 1)
                else:
                    adds(normed=True)

            adds(normed=True)
            mlp(last=False)
            roots()
            act.wait_ge(norm_made, 2)

            def ret_head(i):
                acc_to(0, evac[0][:, :], ACT.Copy, factor(0, rstd))
                split(0, 2)
                batch_qk(0, qkT)
                split(2, 7)
                acc_to(1, evac[1][:, :], ACT.Copy, factor(1, rstd))
                split(7, 8)
                T.up("block")
                batch_qk(1, qkT)
                def high_v(tok):
                    act.wait_ge(acc_done[tok], T("block", 1))
                    act.activation(v_hi[tok], acc[tok][:, :], ACT.Copy,
                                   scale=factor(tok, rstd)).then_inc(v_hi_made[tok], 1)

                high_v(0)
                split(0, 7)
                high_v(1)
                split(7, 8)
                T.up("block")
                act.wait_ge(mixed, T("ret_head", 1))
                for t in range(TOKS):
                    act.activation(gate_r[t], mix[t][:, :], ACT.Square, accum_out=gsum[:, t:t + 1]).then_inc(gsq, 1)
                act.wait_ge(gmean_made, T("ret_head", 1))
                act.activation(groot, gmean, ACT.Sqrt).then_inc(groot_made, 1)
                acc_to(0, gate_r[0], ACT.Silu, factor(0, rstd))
                split(0, 2)
                batch_hi(0, aT_hi, i)
                split(2, 7)
                acc_to(1, gate_r[1], ACT.Silu, factor(1, rstd))
                split(7, 8)
                T.up("block")
                batch_hi(1, aT_hi, i)
                T.up("ret_head")

            for half in range(2):
                T.loop(act, RET_HALF, ret_head, block=3, tr0=2, tr1=2, ret_head=1)
                adds(normed=(half == 1))
            mlp(last=True)

        @block.vector
        def _(dve):
            T = Tally("block", "hi0", "hi1", "step", "norm", "mixer_norm", "group", "ret_head")

            def step(ins):
                ins.then_inc(dve_step, 1)
                T.up("step")
                dve.wait_ge(dve_step, T("step"))

            def split(first, last, block0=False):
                for s in range(first, last):
                    dve.wait_ge(hi_made, s + 1 if block0 else T("block") * SLOTS + (SLOTS + s + 1))
                    c = slice(s * SW, (s + 1) * SW)
                    dve.tensor_tensor(w_lo[:, c], raw[:, s % RAW * SW:(s % RAW + 1) * SW],
                                      w_hi[:, c].bitcast(F32), ALU.subtract).then_inc(lo_made, 1)

            def batch_lo(tok, dst_hi, dst_lo, quad):
                T.up(f"hi{tok}")
                dve.wait_ge(tr_hi[tok], T(f"hi{tok}"))
                c = bass.ds(quad * NB + tok * D, NB)
                dve.tensor_tensor(dst_lo[:, c], tr[tok][:, :], dst_hi[:, c].bitcast(F32),
                                  ALU.subtract).then_inc(tr_out[tok], 1)

            def gained(tok, quad):
                dve.tensor_tensor(stage[tok][:, :], h[:, bass.ds(quad * NB + tok * D, NB)],
                                  gain[:, bass.ds(quad * NB, NB)], ALU.mult).then_inc(staged[tok], 1)

            def mean_squares():
                T.up("norm")
                dve.wait_ge(squared, T("norm") * TOKS * QUADS)
                step(dve.tensor_reduce(mean_sq, sumsq.rearrange("p (t n) -> p t n", t=TOKS), AX_X, ALU.add))
                dve.tensor_scalar(mean_eps, mean_sq, 1.0 / D, EPS, ALU.mult, ALU.add).then_inc(mean_made, 1)
                dve.wait_ge(mean_made, T("norm"))

            def norm_for_mixer():
                mean_squares()
                T.up("mixer_norm")
                dve.wait_ge(root_made, T("mixer_norm"))
                step(dve.reciprocal(rstd, root))
                dve.tensor_scalar(rstd_q, rstd, FOX_DIM ** -0.5, None, ALU.mult).then_inc(norm_made, 1)

            def norm_for_mlp():
                mean_squares()
                step(dve.reciprocal(inv_ms, mean_eps))

            def x_lo(tok, n):
                T.up(f"hi{n % 2}")
                dve.wait_ge(tr_hi[n % 2], T(f"hi{n % 2}"))
                for j in range(NB // P):
                    kt = n * (NB // P) + j
                    c = slice(tok * D + kt * P, tok * D + (kt + 1) * P)
                    ins = dve.scalar_tensor_tensor(xT_lo[:, c], tr[n % 2][:, j * P:(j + 1) * P],
                                                   gain_cols[:, kt:kt + 1], xT_hi[:, c].bitcast(F32),
                                                   ALU.mult, ALU.subtract)
                ins.then_inc(tr_out[n % 2], 1)

            x_lo(0, 0)
            x_lo(0, 1)
            split(0, 1, block0=True)
            x_lo(0, 2)
            split(1, 2, block0=True)
            x_lo(0, 3)
            split(2, 4, block0=True)
            x_lo(1, 0)
            x_lo(1, 1)
            split(4, 5, block0=True)
            x_lo(1, 2)
            x_lo(1, 3)
            split(5, 7, block0=True)
            dve.wait_ge(wf_hi_made, 1)
            wf_hi, wf_lo = (wf_split[:, 0:WF_COLS].rearrange("p (k c h) -> p k c h", k=KT, c=2)[:, :, c, :]
                            for c in range(2))
            dve.tensor_tensor(wf_lo, wf_raw.rearrange("p (k h) -> p k h", k=KT), wf_hi.bitcast(F32),
                              ALU.subtract).then_inc(wf_made, 1)
            split(7, 8, block0=True)
            norm_for_mixer()

            def masked(j):
                head = T("group") * HPG
                b, p, s_bank = 2 * (j % 2), probs[j % 2], sc[j % 2]
                dve.wait_ge(score_done, head + (j + 1))
                if j >= 2:
                    dve.wait_ge(pT_done, head + (j - 1))
                dve.scalar_tensor_tensor(p[:, 0:P], s_bank[:, 0:P], c_group[:, j:j + 1], mask[:, 0:P],
                                         ALU.add, ALU.add)
                step(dve.scalar_tensor_tensor(p[:, P:3 * P], s_bank[:, P:3 * P], c_group[:, HPG + j:HPG + j + 1],
                                              mask[:, P:3 * P], ALU.add, ALU.add))
                dve.tensor_reduce(row_max[:, b:b + 1], p[:, 0:P], AX_X, ALU.max, negate=True)
                dve.tensor_reduce(row_max[:, b + 1:b + 2], p[:, P:3 * P], AX_X, ALU.max,
                                  negate=True).then_inc(score_out, 1)

            def normalised(j):
                b, p = 2 * (j % 2), probs[j % 2]
                dve.wait_ge(exp_made, T("group") * HPG + (j + 1))
                step(dve.reciprocal(row_inv[:, b:b + 2], row_sum[:, b:b + 2]))
                dve.tensor_scalar(p[:, 0:P], p[:, 0:P], row_inv[:, b:b + 1], None, ALU.mult)
                dve.tensor_scalar(p[:, P:3 * P], p[:, P:3 * P], row_inv[:, b + 1:b + 2], None,
                                  ALU.mult).then_inc(probs_made, 1)

            def k_part(middle=None):
                split(0, 5)
                if middle:
                    middle()
                split(5, 8)
                T.up("block")

            def gate_rows_out():
                dve.wait_ge(gate_done, 1)
                dve.tensor_copy(gate_rows, sc[1][0:2 * FOX_HEADS, 0:S]).then_inc(gate_out, 1)

            def log_sigmoid():
                dve.wait_ge(gate_turned, 1)
                dve.wait_ge(bias_in, 16)
                dve.wait_ge(norm_made, 1)
                step(dve.tensor_copy(gate_parts, sc[0][:, 0:TOKS * 2 * FOX_HEADS]))
                parts = gate_parts.rearrange("p (t c h) -> p t c h", t=TOKS, c=2)
                step(dve.tensor_tensor(gate_z.rearrange("p (t h) -> p t h", t=TOKS), parts[:, :, 0, :],
                                       parts[:, :, 1, :], ALU.add))
                for t in range(TOKS):
                    f_cols = slice(t * FOX_HEADS, (t + 1) * FOX_HEADS)
                    step(dve.scalar_tensor_tensor(gate_z[:, f_cols], gate_z[:, f_cols], rstd[:, t:t + 1], bias_f,
                                                  ALU.mult, ALU.add))
                dve.scalar_tensor_tensor(gate_a, gate_z, -1.0, gate_z, ALU.mult, ALU.max).then_inc(gate_zed, 1)
                step(dve.tensor_scalar(gate_m, gate_z, 0.0, None, ALU.min))
                dve.wait_ge(gate_ln, 1)
                step(dve.tensor_tensor(log_f[:, :], gate_m, gate_l, ALU.subtract))

            def q_and_v(g):
                f_group = log_f_group[:, :].rearrange("p (t r) -> p t r", t=TOKS)
                f = log_f[:, :].rearrange("p (t h) -> p t h", t=TOKS)[:, :, bass.ds(g * HPG, HPG)]
                dve.tensor_copy(f_group[:, :, 0:HPG], f)
                dve.tensor_copy(f_group[:, :, LO_ROW:C_ROWS], f).then_inc(cum_src, 1)
                split(0, 4)
                dve.wait_ge(cum_done, T("group", 1))
                dve.tensor_copy(c_group, sc[0][:, 0:TOKS * HPG])
                dve.tensor_scalar(negc[:, P:3 * P], sc[0][0:C_ROWS, P:3 * P], -1.0, None, ALU.mult)
                step(dve.tensor_scalar(negc[:, 0:P], sc[0][0:C_ROWS, P:2 * P], -1.0, None, ALU.mult))
                low = slice(LO_ROW, C_ROWS)
                dve.scalar_tensor_tensor(negc[low, P:3 * P], sc[0][low, P:3 * P], -1.0, negc[low, P:3 * P].bitcast(F32),
                                         ALU.mult, ALU.subtract)
                dve.scalar_tensor_tensor(negc[low, 0:P], sc[0][low, P:2 * P], -1.0, negc[low, 0:P].bitcast(F32),
                                         ALU.mult, ALU.subtract).then_inc(cum_out, 1)
                dve.wait_ge(cum_out, T("group", 1))
                split(4, 8)
                T.up("block")
                masked(0)
                normalised(0)
                masked(1)
                normalised(1)
                masked(2)
                normalised(2)
                masked(3)
                split(0, 1)
                normalised(3)
                split(1, 4)
                batch_lo(0, aT_hi, aT_lo, g)
                split(4, 8)
                T.up("block")
                T.up("group")
                batch_lo(1, aT_hi, aT_lo, g)

            def group_and_k(g):
                q_and_v(g)
                k_part()

            k_part(gate_rows_out)
            log_sigmoid()
            dve.wait_ge(const_in, 16)
            dve.wait_ge(zeros_set, 2)
            dve.tensor_copy(pick, const[0:C_ROWS, C_PICK:C_PICK + HPG])
            T.loop(dve, GROUPS - 1, group_and_k, block=3, hi0=1, hi1=1, step=2 * HPG + 1, group=1)
            q_and_v(GROUPS - 1)

            def add(tok, n, scale):
                dve.wait_ge(acc_done[tok], T("block", 1))
                h_cols = h[:, bass.ds(n * NB + tok * D, NB)]
                if scale is None:
                    ins = dve.tensor_tensor(h_cols, acc[tok][:, :], h_cols, ALU.add)
                else:
                    ins = dve.scalar_tensor_tensor(h_cols, acc[tok][:, :], scale[:, tok:tok + 1], h_cols,
                                                   ALU.mult, ALU.add)
                ins.then_inc(acc_out[tok], 1)

            def add_block(n, scale, batches=False, feeds=True):
                add(0, n, scale)
                if batches:
                    dve.wait_ge(acc_out[0], T("block", 1))
                    gained(0, n)
                if feeds:
                    split(0, 2)
                if batches:
                    batch_lo(0, xT_hi, xT_lo, n)
                if feeds:
                    split(2, 7)
                add(1, n, scale)
                if batches:
                    dve.wait_ge(acc_out[1], T("block", 1))
                    gained(1, n)
                if feeds:
                    split(7, 8)
                T.up("block")
                if batches:
                    batch_lo(1, xT_hi, xT_lo, n)

            def adds(scale, batches):
                if batches:
                    dve.wait_ge(gain_in, T("norm") * 16)
                    T.loop(dve, QUADS, lambda n: add_block(n, scale, True), block=1, hi0=1, hi1=1)
                else:
                    T.loop(dve, QUADS, lambda n: add_block(n, scale), block=1)

            def up_block(u):
                def squares(tok):
                    dve.wait_ge(acc_out[tok], T("block", 1))
                    dve.tensor_tensor(stage[tok][:, :], evac[tok][:, :], evac[tok][:, :],
                                      ALU.mult).then_inc(staged[tok], 1)
                squares(0)
                split(0, 2)
                batch_lo(0, aT_hi, aT_lo, u)
                split(2, 7)
                squares(1)
                split(7, 8)
                T.up("block")
                batch_lo(1, aT_hi, aT_lo, u)

            def mlp(last):
                norm_for_mlp()

                def ups():
                    T.loop(dve, QUADS, up_block, block=1, hi0=1, hi1=1)

                def chunk(i):
                    ups()
                    adds(inv_ms, False)

                T.loop(dve, SUPER - 1, chunk, block=2 * QUADS, hi0=QUADS, hi1=QUADS)
                ups()
                if last:
                    T.loop(dve, QUADS - 1, lambda n: add_block(n, inv_ms), block=1)
                else:
                    adds(inv_ms, True)

            adds(None, True)
            mlp(last=False)
            norm_for_mixer()

            def rotated(tok):
                dve.wait_ge(acc_out[tok], T("block", 1))
                e = evac[tok][:, :].rearrange("p (m f d) -> p m f d", m=2, f=2)
                o = stage[tok][:, :].rearrange("p (m f d) -> p m f d", m=2, f=2)
                r = [rot[:, k * S:(k + 1) * S].rearrange("p (m d) -> p m d", m=2) for k in range(4)]
                cos, sin = (const[:, c + tok * P:c + (tok + 1) * P].unsqueeze(1).broadcast_to([P, 2, P])
                            for c in (C_COS, C_SIN))
                dve.tensor_tensor(r[0], e[:, :, 0, :], cos, ALU.mult)
                dve.tensor_tensor(r[1], e[:, :, 1, :], sin, ALU.mult)
                dve.tensor_tensor(r[2], e[:, :, 0, :], sin, ALU.mult)
                step(dve.tensor_tensor(r[3], e[:, :, 1, :], cos, ALU.mult))
                dve.tensor_tensor(o[:, :, 0, :], r[0], r[1], ALU.subtract)
                dve.tensor_tensor(o[:, :, 1, :], r[2], r[3], ALU.add).then_inc(staged[tok], 1)

            def gated_out(tok):
                dve.wait_ge(gated[tok], T("ret_head", 1))
                dve.scalar_tensor_tensor(stage[tok][:, :], mix[tok][:, :], grstd[:, tok:tok + 1], gate_r[tok],
                                         ALU.mult, ALU.mult).then_inc(staged[tok], 1)

            def ret_head(i):
                rotated(0)
                split(0, 7)
                rotated(1)
                split(7, 8)
                T.up("block")
                def low_v(tok):
                    dve.wait_ge(v_hi_made[tok], T("ret_head", 1))
                    dve.scalar_tensor_tensor(v_lo[tok], acc[tok][:, :], rstd[:, tok:tok + 1], v_hi[tok].bitcast(F32),
                                             ALU.mult, ALU.subtract).then_inc(acc_out[tok], 1)

                low_v(0)
                split(0, 4)
                dve.wait_ge(score_done, T("ret_head") + (FOX_HEADS + 1))
                dve.wait_ge(table_in, T("ret_head") * 32 + 32)
                step(dve.tensor_tensor(inner, sc[0][:, 0:3 * P], decay_t, ALU.mult))
                step(dve.tensor_copy(inner_hi, inner))
                dve.tensor_tensor(inner_lo, inner, inner_hi.bitcast(F32), ALU.subtract).then_inc(inner_made, 1)
                split(4, 7)
                low_v(1)
                split(7, 8)
                T.up("block")
                dve.wait_ge(gsq, T("ret_head") * TOKS + TOKS)
                dve.tensor_scalar(gmean, gsum, 1.0 / RET_V, EPS, ALU.mult, ALU.add).then_inc(gmean_made, 1)
                dve.wait_ge(groot_made, T("ret_head", 1))
                step(dve.reciprocal(grstd, groot))
                gated_out(0)
                split(0, 2)
                batch_lo(0, aT_hi, aT_lo, i)
                split(2, 7)
                gated_out(1)
                split(7, 8)
                T.up("block")
                batch_lo(1, aT_hi, aT_lo, i)
                T.up("ret_head")

            for half in range(2):
                T.loop(dve, RET_HALF, ret_head, block=3, hi0=1, hi1=1, step=5, ret_head=1)
                adds(None, half == 1)
            mlp(last=True)

            def final_gain(t, n):
                c = slice(t * D + n * NB, t * D + (n + 1) * NB)
                return dve.tensor_tensor(y[:, c], h[:, c], gain[:, n * NB:(n + 1) * NB], ALU.mult)

            dve.wait_ge(gain_in, 16 * 4)
            dve.wait_ge(lo_made, BLOCKS * SLOTS)
            for t in range(TOKS):
                dve.wait_ge(acc_out[t], T("block"))
                for n in range(QUADS - 1):
                    final_gain(t, n)
            for t in range(TOKS):
                col = slice(t, t + 1)
                add(t, QUADS - 1, inv_ms)
                dve.wait_ge(acc_out[t], T("block", 1))
                step(final_gain(t, QUADS - 1))
                dve.wait_ge(squared, T("norm") * TOKS * QUADS + TOKS * (QUADS - 1) + 1 + t)
                step(dve.tensor_reduce(mean_tok[:, col], sumsq[:, t * QUADS:(t + 1) * QUADS], AX_X, ALU.add))
                dve.tensor_scalar(mean_eps_tok[:, col], mean_tok[:, col], 1.0 / D, EPS, ALU.mult,
                                  ALU.add).then_inc(mean_made, 1)
                dve.wait_ge(root_made, T("mixer_norm", 1 + t))
                dve.reciprocal(rstd_tok[:, col], root_tok[:, col]).then_inc(norm_made, 1)
                dve.wait_ge(norm_made, T("mixer_norm", 1 + t))
                pieces = [slice(0, D)] if t == 0 else [slice(D + n * NB, D + (n + 1) * NB) for n in range(QUADS // 2)]
                for c in pieces:
                    dve.tensor_scalar(y[:, c], y[:, c], rstd_tok[:, col], None, ALU.mult).then_inc(scaled_dve, 1)


def weight_stream(fox_wk, fox_wq, fox_wv, fox_wo, ret_wq, ret_wk, ret_wv, ret_wg, ret_wo, mlp_up, mlp_down):
    import numpy as np

    stream = np.empty((BLOCKS, SLOTS, P, PER_SLOT, NB), np.float32)
    count = 0

    def put(*parts):
        nonlocal count
        at = 0
        for w in parts:
            n = w.shape[1]
            stream[count, :, :, :, at:at + n] = w.reshape(SLOTS, PER_SLOT, P, n).transpose(0, 2, 1, 3)
            at += n
        count += 1

    def mlp(up, down):
        for c in range(SUPER):
            for u in range(QUADS):
                put(up[:, c * D + u * NB:c * D + (u + 1) * NB])
            for n in range(QUADS):
                put(down[c * D:(c + 1) * D, n * NB:(n + 1) * NB])

    for g in range(GROUPS):
        for w in (fox_wk, fox_wq, fox_wv):
            put(w[:, g * NB:(g + 1) * NB])
    for n in range(QUADS):
        put(fox_wo[:, n * NB:(n + 1) * NB])
    mlp(mlp_up[0], mlp_down[0])
    for half in range(2):
        for hd in range(half * RET_HALF, (half + 1) * RET_HALF):
            qk = slice(hd * RET_QK, (hd + 1) * RET_QK)
            v = slice(hd * RET_V, (hd + 1) * RET_V)
            put(ret_wq[:, qk], ret_wk[:, qk])
            put(ret_wv[:, v])
            put(ret_wg[:, v])
        for n in range(QUADS):
            put(ret_wo[half * D:(half + 1) * D, n * NB:(n + 1) * NB])
    mlp(mlp_up[1], mlp_down[1])
    assert count == BLOCKS
    return stream.reshape(BLOCKS, SLOTS, P, SW)


def shape_constants():
    import numpy as np

    table = np.zeros((P, C_END), np.float32)
    i = np.arange(P)
    table[:, C_ID:C_ID + P] = np.eye(P)
    table[:, C_TRI:C_TRI + P] = i[:, None] <= i[None, :]
    table[:, C_ONE:C_ONE + P] = 1.0
    diagonal = np.where(i[None, :] <= i[:, None], 0.0, MASKED)
    table[:, C_MASK:C_MASK + P] = diagonal
    table[:, C_MASK + 2 * P:C_MASK + 3 * P] = diagonal
    half = RET_QK // 2
    inv = np.float32(10000.0) ** (-np.arange(half, dtype=np.float32) / np.float32(half))
    for t in range(TOKS):
        angle = (np.float32(t * P) + i.astype(np.float32))[:, None] * inv[None, :]
        table[:, C_COS + t * P:C_COS + (t + 1) * P] = np.cos(angle)
        table[:, C_SIN + t * P:C_SIN + (t + 1) * P] = np.sin(angle)
    table[i[:HPG], C_PICK + i[:HPG]] = 1.0
    table[LO_ROW + i[:HPG], C_PICK + i[:HPG]] = 1.0
    log_gamma = np.log1p(-np.exp2(-5.0 - np.arange(RET_HEADS, dtype=np.float64)))
    diff = (i[None, :] - i[:, None]).astype(np.float64)
    decay = np.zeros((RET_HEADS, P, 3 * P), np.float32)
    for hd in range(RET_HEADS):
        same = np.where(diff >= 0, np.exp(log_gamma[hd] * np.maximum(diff, 0.0)), 0.0) * RET_QK ** -0.5
        decay[hd, :, 0:P] = same
        decay[hd, :, P:2 * P] = np.exp(log_gamma[hd] * (diff + P)) * RET_QK ** -0.5
        decay[hd, :, 2 * P:] = same
    return table, decay


def kernel(x, fox_norm, fox_wq, fox_wk, fox_wv, fox_wf, fox_bf, fox_wo, ret_norm, ret_wq, ret_wk, ret_wv,
           ret_wg, ret_gn, ret_wo, mlp_norm, mlp_up, mlp_down, final_norm):
    import numpy as np
    import concourse.bacc as bacc
    from concourse.bass_utils import run_bass_kernel_spmd

    a = np.asarray
    rows = lambda v: np.broadcast_to(a(v)[..., None, :], a(v).shape[:-1] + (P, a(v).shape[-1]))
    table, decay = shape_constants()
    arrays = {
        "x": np.ascontiguousarray(a(x)[0]),
        "w_stream": weight_stream(
            a(fox_wk)[0], a(fox_wq)[0], a(fox_wv)[0], a(fox_wo)[0], a(ret_wq)[0], a(ret_wk)[0], a(ret_wv)[0],
            a(ret_wg)[0], a(ret_wo)[0], a(mlp_up), a(mlp_down)),
        "gain_t": np.ascontiguousarray(a(fox_norm)[0].reshape(KT, P).T),
        "gains": np.ascontiguousarray(np.stack([
            rows(mlp_norm)[0], rows(ret_norm)[0], rows(mlp_norm)[1], rows(final_norm)])),
        "gn": np.ascontiguousarray(rows(a(ret_gn)[0].reshape(RET_HEADS, RET_V))),
        "wf": np.ascontiguousarray(a(fox_wf)[0].reshape(KT, P, FOX_HEADS).transpose(1, 0, 2).reshape(P, -1)),
        "bf": np.ascontiguousarray(rows(fox_bf)[0]),
        "consts": table,
        "decay": decay,
    }
    nc = bacc.Bacc("TRN2", target_bir_lowering=False, num_devices=1)
    ins = [nc.dram_tensor(f"in_{n}", v.shape, F32, kind="ExternalInput").ap() for n, v in arrays.items()]
    out = nc.dram_tensor("out", (S, D), F32, kind="ExternalOutput").ap()
    build_trunk(nc, *ins, out)
    r = run_bass_kernel_spmd(nc, [{f"in_{n}": v for n, v in arrays.items()}], core_ids=[0])
    return r.results[0]["out"].reshape(1, S, D)
```
